# Optimizing a Trainium2 kernel written in Bass

```python
import jax, jax.numpy as jnp
from jax import lax
import numpy as np

D_MODEL = 1024
BATCH = 1
SEQ = 256
DEPTH = 2

MLA_HEADS = 4
QK_NOPE_DIM = 128
QK_ROPE_DIM = 64
QK_HEAD_DIM = QK_NOPE_DIM + QK_ROPE_DIM
V_HEAD_DIM = 128
Q_LORA_RANK = 256
KV_LORA_RANK = 128
ROPE_THETA = 10000.0
SB_HEADS = 4
SB_HEAD_DIM = 128
D_FF = 2816
CONV_WIDTH = 3
BLOCK_Q = 128
SUB = 16
N_SUB = BLOCK_Q // SUB
EPS = 1e-6
N_MOD = 6

MLA_WIDTH = MLA_HEADS * V_HEAD_DIM
SB_WIDTH = SB_HEADS * SB_HEAD_DIM
IN_SPLITS = (Q_LORA_RANK, KV_LORA_RANK, QK_ROPE_DIM, SB_WIDTH, SB_WIDTH, SB_WIDTH, D_MODEL, D_MODEL)
D_IN = sum(IN_SPLITS)
IN_SPLIT_POINTS = [sum(IN_SPLITS[:i + 1]) for i in range(len(IN_SPLITS) - 1)]


def rms_norm(x, g):
    x32 = x.astype(jnp.float32)
    y = x32 * lax.rsqrt(jnp.mean(x32 * x32, axis=-1, keepdims=True) + EPS)
    return (y * g.astype(jnp.float32)).astype(x.dtype)

def rope(x, positions):
    dr = x.shape[-1]
    half = dr // 2
    inv_freq = 1.0 / (ROPE_THETA ** (jnp.arange(half, dtype=jnp.float32) * (2.0 / dr)))
    ang = positions.astype(jnp.float32)[..., None] * inv_freq
    ang = ang.reshape(ang.shape[:2] + (1,) * (x.ndim - 3) + (half,))
    cos, sin = jnp.cos(ang), jnp.sin(ang)
    x32 = x.astype(jnp.float32)
    x1, x2 = x32[..., :half], x32[..., half:]
    return jnp.concatenate([x1 * cos - x2 * sin, x2 * cos + x1 * sin], axis=-1).astype(x.dtype)

def causal_softmax_attention(q, k, v):
    b, s, h, _ = q.shape
    scale = QK_HEAD_DIM ** -0.5
    qh = q.transpose(0, 2, 1, 3).astype(jnp.float32)
    kh = k.transpose(0, 2, 1, 3).astype(jnp.float32)
    vh = v.transpose(0, 2, 1, 3).astype(jnp.float32)
    outs = []
    for i in range(s // BLOCK_Q):
        st = i * BLOCK_Q
        ln = st + BLOCK_Q
        sc = jnp.einsum('bhqd,bhkd->bhqk', qh[:, :, st:ln], kh[:, :, :ln]) * scale
        mask = np.arange(ln)[None, :] <= np.arange(st, ln)[:, None]
        p = jax.nn.softmax(jnp.where(mask, sc, -jnp.inf), axis=-1)
        outs.append(jnp.einsum('bhqk,bhkd->bhqd', p, vh[:, :, :ln]))
    o = jnp.concatenate(outs, axis=2)
    return o.transpose(0, 2, 1, 3).reshape(b, s, h * v.shape[-1]).astype(v.dtype)

def reverse_cumsum_keys(l):
    lead = l.shape[:-1]
    nk = l.shape[-1] // BLOCK_Q
    r = l.reshape(lead + (nk, N_SUB, SUB))
    c0 = lax.cumsum(r, axis=r.ndim - 1, reverse=True)
    s0 = c0[..., 0]
    c1 = lax.cumsum(s0, axis=s0.ndim - 1, reverse=True)
    s1 = c1[..., 0]
    c2 = lax.cumsum(s1, axis=s1.ndim - 1, reverse=True) - s1
    tot = c0 + (c1 - s0)[..., None] + c2[..., None, None]
    return tot.reshape(l.shape)

def stick_breaking_attention(q, k, v):
    b, s, h, d = q.shape
    scale = d ** -0.5
    qh = q.transpose(0, 2, 1, 3).astype(jnp.float32)
    kh = k.transpose(0, 2, 1, 3).astype(jnp.float32)
    vh = v.transpose(0, 2, 1, 3).astype(jnp.float32)
    outs = []
    for i in range(s // BLOCK_Q):
        st = i * BLOCK_Q
        ln = st + BLOCK_Q
        z = jnp.einsum('bhqd,bhkd->bhqk', qh[:, :, st:ln], kh[:, :, :ln]) * scale
        past = np.arange(ln)[None, :] < np.arange(st, ln)[:, None]
        l = jnp.where(past, jax.nn.log_sigmoid(-z), 0.0)
        a = jnp.where(past, jnp.exp(z + reverse_cumsum_keys(l)), 0.0)
        outs.append(jnp.einsum('bhqk,bhkd->bhqd', a, vh[:, :, :ln]))
    o = jnp.concatenate(outs, axis=2)
    return o.transpose(0, 2, 1, 3).reshape(b, s, h * d).astype(v.dtype)

def causal_depthwise_conv(u, w, bias):
    ch = u.shape[-1]
    out = lax.conv_general_dilated(
        u, w[:, None, :].astype(u.dtype), window_strides=(1,),
        padding=[(CONV_WIDTH - 1, 0)], dimension_numbers=('NWC', 'WIO', 'NWC'),
        feature_group_count=ch)
    return out + bias

def first_inputs(seed: int = 0) -> dict:
    key = jax.random.key(seed)
    ks = jax.random.split(key, 24)
    f32 = jnp.float32

    def nrm(k, shape, scale):
        return jax.random.normal(k, shape, f32) * scale

    def gain(k, n):
        return 1.0 + 0.02 * jax.random.normal(k, (DEPTH, n), f32)

    return {
        "x": nrm(ks[0], (BATCH, SEQ, D_MODEL), 1.0),
        "c": nrm(ks[1], (BATCH, D_MODEL), 1.0),
        "positions": jnp.broadcast_to(jnp.arange(SEQ, dtype=jnp.int32)[None, :], (BATCH, SEQ)),
        "w_ada": nrm(ks[2], (DEPTH, D_MODEL, N_MOD * D_MODEL), 0.5 * D_MODEL ** -0.5),
        "b_ada": nrm(ks[3], (DEPTH, N_MOD * D_MODEL), 0.02),
        "g_norm1": gain(ks[4], D_MODEL),
        "w_in": nrm(ks[5], (DEPTH, D_MODEL, D_IN), D_MODEL ** -0.5),
        "b_in": nrm(ks[6], (DEPTH, D_IN), 0.02),
        "g_q_lat": gain(ks[7], Q_LORA_RANK),
        "w_uq": nrm(ks[8], (DEPTH, Q_LORA_RANK, MLA_HEADS * QK_HEAD_DIM), Q_LORA_RANK ** -0.5),
        "g_kv_lat": gain(ks[9], KV_LORA_RANK),
        "w_ukv": nrm(ks[10], (DEPTH, KV_LORA_RANK, MLA_HEADS * (QK_NOPE_DIM + V_HEAD_DIM)), KV_LORA_RANK ** -0.5),
        "g_q_head": gain(ks[11], QK_HEAD_DIM),
        "g_k_head": gain(ks[12], QK_HEAD_DIM),
        "w_branch_mla": nrm(ks[13], (DEPTH, MLA_WIDTH, D_MODEL), MLA_WIDTH ** -0.5),
        "w_branch_sb": nrm(ks[14], (DEPTH, SB_WIDTH, D_MODEL), SB_WIDTH ** -0.5),
        "w_out": nrm(ks[15], (DEPTH, D_MODEL, D_MODEL), D_MODEL ** -0.5),
        "g_norm2": gain(ks[16], D_MODEL),
        "w_up": nrm(ks[17], (DEPTH, D_MODEL, 2 * D_FF), D_MODEL ** -0.5),
        "w_conv": nrm(ks[18], (DEPTH, CONV_WIDTH, 2 * D_FF), CONV_WIDTH ** -0.5),
        "b_conv": nrm(ks[19], (DEPTH, 2 * D_FF), 0.02),
        "w_down": nrm(ks[20], (DEPTH, D_FF, D_MODEL), D_FF ** -0.5),
    }

def first_block(x, c, positions, w_ada, b_ada, g_norm1, w_in, b_in, g_q_lat, w_uq, g_kv_lat,
              w_ukv, g_q_head, g_k_head, w_branch_mla, w_branch_sb, w_out, g_norm2, w_up,
              w_conv, b_conv, w_down):
    b, s, _ = x.shape
    c_act = jax.nn.silu(c)
    for l in range(DEPTH):
        mod = c_act @ w_ada[l] + b_ada[l]
        sh1, sc1, gt1, sh2, sc2, gt2 = [m[:, None, :] for m in jnp.split(mod, N_MOD, axis=-1)]

        h = rms_norm(x, g_norm1[l]) * (1.0 + sc1) + sh1
        u = h @ w_in[l] + b_in[l]
        q_lat, kv_lat, k_rope, q_sb, k_sb, v_sb, gate_mla, gate_sb = jnp.split(u, IN_SPLIT_POINTS, axis=-1)

        q = (rms_norm(q_lat, g_q_lat[l]) @ w_uq[l]).reshape(b, s, MLA_HEADS, QK_HEAD_DIM)
        kv = (rms_norm(kv_lat, g_kv_lat[l]) @ w_ukv[l]).reshape(b, s, MLA_HEADS, QK_NOPE_DIM + V_HEAD_DIM)
        k_nope, v_mla = kv[..., :QK_NOPE_DIM], kv[..., QK_NOPE_DIM:]
        k_rope_h = jnp.broadcast_to(k_rope[:, :, None, :], (b, s, MLA_HEADS, QK_ROPE_DIM))
        k = jnp.concatenate([k_nope, k_rope_h], axis=-1)
        q = rms_norm(q, g_q_head[l])
        k = rms_norm(k, g_k_head[l])
        q = jnp.concatenate([q[..., :QK_NOPE_DIM], rope(q[..., QK_NOPE_DIM:], positions)], axis=-1)
        k = jnp.concatenate([k[..., :QK_NOPE_DIM], rope(k[..., QK_NOPE_DIM:], positions)], axis=-1)
        y_mla = causal_softmax_attention(q, k, v_mla)

        y_sb = stick_breaking_attention(
            q_sb.reshape(b, s, SB_HEADS, SB_HEAD_DIM),
            k_sb.reshape(b, s, SB_HEADS, SB_HEAD_DIM),
            v_sb.reshape(b, s, SB_HEADS, SB_HEAD_DIM))

        merged = (jax.nn.sigmoid(gate_mla) * (y_mla @ w_branch_mla[l])
                  + jax.nn.sigmoid(gate_sb) * (y_sb @ w_branch_sb[l]))
        x = x + gt1 * (merged @ w_out[l])

        h = rms_norm(x, g_norm2[l]) * (1.0 + sc2) + sh2
        up = causal_depthwise_conv(h @ w_up[l], w_conv[l], b_conv[l])
        a, v_ff = jnp.split(up, 2, axis=-1)
        x = x + gt2 * ((jax.nn.silu(a) * v_ff) @ w_down[l])
    return x


GRID_W = 64
CTX_LEN = 256
HEAD_DIM = 64
N_HEADS_A = 8
N_KV_A = 2
N_HEADS_B = 8
N_KV_B = 2
BRANCH_WIDTH = 512
CONV_K = 3
WINDOW = 128
Q_BLOCK = 128
N_BRANCH = 3
N_EXPERTS = 16
EXPERT_HIDDEN = 1024
CAPACITY_FACTOR = 2
ROPE_BASE = 10000.0
NEG_INF = -1e30

KV_A = N_KV_A * HEAD_DIM
KV_B = N_KV_B * HEAD_DIM
KV_END = 2 * KV_A + 2 * KV_B
OFF_QA = KV_END
OFF_QB = OFF_QA + N_HEADS_A * HEAD_DIM
OFF_CONV = OFF_QB + N_HEADS_B * HEAD_DIM
OFF_GATE = OFF_CONV + 3 * BRANCH_WIDTH
PROJ_WIDTH = OFF_GATE + N_BRANCH * D_MODEL


def rmsnorm(x, g):
    x32 = x.astype(jnp.float32)
    y = x32 * lax.rsqrt(jnp.mean(x32 * x32, axis=-1, keepdims=True) + EPS)
    return (y * g.astype(jnp.float32)).astype(x.dtype)

def modulate(h, shift, scale):
    return h * (1 + scale) + shift

def rope_tables(n):
    rows = n // GRID_W
    row = jnp.repeat(jnp.arange(rows, dtype=jnp.float32), GRID_W)
    col = jnp.tile(jnp.arange(GRID_W, dtype=jnp.float32), rows)
    n_freq = HEAD_DIM // 4
    inv = ROPE_BASE ** (-jnp.arange(n_freq, dtype=jnp.float32) / n_freq)
    ang = jnp.concatenate([row[:, None] * inv, col[:, None] * inv], axis=-1)
    return jnp.cos(ang), jnp.sin(ang)

def apply_rope(x, cos, sin):
    half = HEAD_DIM // 2
    c = cos[None, :, None, :].astype(x.dtype)
    s = sin[None, :, None, :].astype(x.dtype)
    x1, x2 = x[..., :half], x[..., half:]
    return jnp.concatenate([x1 * c - x2 * s, x2 * c + x1 * s], axis=-1)

def q_heads(p_q, qg, n_heads, n_kv, rope):
    B, n, _ = p_q.shape
    q = rmsnorm(p_q.reshape(B, n, n_heads, HEAD_DIM), qg)
    if rope is not None:
        q = apply_rope(q, *rope)
    return q.reshape(B, n, n_kv, n_heads // n_kv, HEAD_DIM)

def kv_heads(p_kv, kg_a, kg_b, rope):
    B, n, _ = p_kv.shape
    ka, va, kb, vb = jnp.split(p_kv, [KV_A, 2 * KV_A, 2 * KV_A + KV_B], axis=-1)
    ka = rmsnorm(ka.reshape(B, n, N_KV_A, HEAD_DIM), kg_a)
    kb = rmsnorm(kb.reshape(B, n, N_KV_B, HEAD_DIM), kg_b)
    va = va.reshape(B, n, N_KV_A, HEAD_DIM)
    vb = vb.reshape(B, n, N_KV_B, HEAD_DIM)
    if rope is not None:
        ka = apply_rope(ka, *rope)
        kb = apply_rope(kb, *rope)
    return ka, va, kb, vb

def attend(q, k, v, mask, sink):
    s = jnp.einsum('bqkgd,bskd->bkgqs', q, k, preferred_element_type=jnp.float32) * (HEAD_DIM ** -0.5)
    if mask is not None:
        s = jnp.where(mask, s, NEG_INF)
    if sink is not None:
        sk = jnp.broadcast_to(sink.astype(jnp.float32)[None, :, :, None, None], s.shape[:-1] + (1,))
        p = jax.nn.softmax(jnp.concatenate([s, sk], axis=-1), axis=-1)[..., :-1]
    else:
        p = jax.nn.softmax(s, axis=-1)
    return jnp.einsum('bkgqs,bskd->bqkgd', p.astype(v.dtype), v)

def to_blocks(q):
    B, n, KV, G, d = q.shape
    return q.reshape(B, n // Q_BLOCK, Q_BLOCK, KV, G, d).transpose(1, 0, 2, 3, 4, 5)

def from_blocks(o, n):
    nblk, B, qb, KV, G, d = o.shape
    return o.transpose(1, 0, 2, 3, 4, 5).reshape(B, n, KV * G * d)

def global_attention(q, k_lat, v_lat, k_ctx, v_ctx):
    k = jnp.concatenate([k_lat, k_ctx], axis=1)
    v = jnp.concatenate([v_lat, v_ctx], axis=1)
    o = lax.map(lambda qb: attend(qb, k, v, None, None), to_blocks(q))
    return from_blocks(o, q.shape[1])

def window_attention(q, k_lat, v_lat, k_ctx, v_ctx, sink):
    n = q.shape[1]
    nblk = n // Q_BLOCK
    pad = ((0, 0), (WINDOW, WINDOW), (0, 0), (0, 0))
    k_pad = jnp.pad(k_lat, pad)
    v_pad = jnp.pad(v_lat, pad)
    span = Q_BLOCK + 2 * WINDOW
    ctx_mask = jnp.ones((Q_BLOCK, k_ctx.shape[1]), dtype=bool)

    def block(args):
        i, qb = args
        start = i * Q_BLOCK
        kb = lax.dynamic_slice_in_dim(k_pad, start, span, axis=1)
        vb = lax.dynamic_slice_in_dim(v_pad, start, span, axis=1)
        qpos = start + jnp.arange(Q_BLOCK)
        kpos = start - WINDOW + jnp.arange(span)
        local = (jnp.abs(qpos[:, None] - kpos[None, :]) <= WINDOW) & (kpos >= 0)[None, :] & (kpos < n)[None, :]
        mask = jnp.concatenate([local, ctx_mask], axis=1)
        return attend(qb, jnp.concatenate([kb, k_ctx], axis=1), jnp.concatenate([vb, v_ctx], axis=1), mask, sink)

    o = lax.map(block, (jnp.arange(nblk), to_blocks(q)))
    return from_blocks(o, n)

def short_conv(p_conv, w):
    b_gate, c_gate, x_in = jnp.split(p_conv, 3, axis=-1)
    u = c_gate * x_in
    n = u.shape[1]
    up = jnp.pad(u, ((0, 0), (CONV_K // 2, CONV_K // 2), (0, 0)))
    conv = sum(w[j] * up[:, j:j + n] for j in range(CONV_K))
    return b_gate * conv

def merge_branches(o_a, o_b, o_c, gate_logits, w_branch, w_out):
    g_a, g_b, g_c = jnp.split(jax.nn.sigmoid(gate_logits), 3, axis=-1)
    merged = g_a * (o_a @ w_branch[0]) + g_b * (o_b @ w_branch[1]) + g_c * (o_c @ w_branch[2])
    return merged @ w_out

def latent_mixer(p, ctx_kv, rope, qg_a, kg_a, qg_b, kg_b, sink, conv_w, w_branch, w_out):
    ka, va, kb, vb = kv_heads(p[..., :KV_END], kg_a, kg_b, rope)
    ka_c, va_c, kb_c, vb_c = ctx_kv
    qa = q_heads(p[..., OFF_QA:OFF_QB], qg_a, N_HEADS_A, N_KV_A, rope)
    qb = q_heads(p[..., OFF_QB:OFF_CONV], qg_b, N_HEADS_B, N_KV_B, rope)
    o_a = global_attention(qa, ka, va, ka_c, va_c)
    o_b = window_attention(qb, kb, vb, kb_c, vb_c, sink.reshape(N_KV_B, N_HEADS_B // N_KV_B))
    o_c = short_conv(p[..., OFF_CONV:OFF_GATE], conv_w)
    return merge_branches(o_a, o_b, o_c, p[..., OFF_GATE:], w_branch, w_out)

def context_mixer(pc, ctx_kv, qg_a, qg_b, sink, conv_w, w_branch, w_out):
    B, L, _ = pc.shape
    ka_c, va_c, kb_c, vb_c = ctx_kv
    qa = q_heads(pc[..., OFF_QA:OFF_QB], qg_a, N_HEADS_A, N_KV_A, None)
    qb = q_heads(pc[..., OFF_QB:OFF_CONV], qg_b, N_HEADS_B, N_KV_B, None)
    o_a = attend(qa, ka_c, va_c, None, None).reshape(B, L, -1)
    o_b = attend(qb, kb_c, vb_c, None, sink.reshape(N_KV_B, N_HEADS_B // N_KV_B)).reshape(B, L, -1)
    o_c = short_conv(pc[..., OFF_CONV:OFF_GATE], conv_w)
    return merge_branches(o_a, o_b, o_c, pc[..., OFF_GATE:], w_branch, w_out)

def expert_choice_ffn(h, w_router, w_g, w_u, w_d):
    B, n, D = h.shape
    cap = CAPACITY_FACTOR * n // N_EXPERTS
    logits = jnp.einsum('bnd,de->ben', h, w_router, preferred_element_type=jnp.float32)
    aff = jax.nn.softmax(logits, axis=1)
    gate, idx = lax.top_k(aff, cap)
    bi = jnp.arange(B)[:, None, None]
    xs = h[bi, idx]
    a = jnp.einsum('becd,edf->becf', xs, w_g)
    u = jnp.einsum('becd,edf->becf', xs, w_u)
    y = jnp.einsum('becf,efd->becd', jax.nn.silu(a) * u, w_d)
    return jnp.zeros_like(h).at[bi, idx].add(y * gate[..., None].astype(y.dtype))

def second_inputs(seed: int = 0) -> dict:
    key = jax.random.key(seed)
    ks = jax.random.split(key, 22)
    D = D_MODEL

    def nrm(k, shape, scale):
        return jax.random.normal(k, shape, jnp.float32) * scale

    return {
        "x": nrm(ks[0], (BATCH, SEQ, D), 1.0),
        "c": nrm(ks[1], (BATCH, D), 1.0),
        "ctx": nrm(ks[2], (BATCH, CTX_LEN, D), 1.0),
        "c_ctx": nrm(ks[3], (D,), 1.0),
        "w_ada": nrm(ks[4], (DEPTH, D, 6 * D), 0.5 * D ** -0.5),
        "b_ada": nrm(ks[5], (DEPTH, 6 * D), 0.02),
        "g_mix": 1.0 + nrm(ks[6], (DEPTH, D), 0.02),
        "g_ffn": 1.0 + nrm(ks[7], (DEPTH, D), 0.02),
        "w_in": nrm(ks[8], (DEPTH, D, PROJ_WIDTH), D ** -0.5),
        "qg_a": 1.0 + nrm(ks[9], (DEPTH, HEAD_DIM), 0.02),
        "kg_a": 1.0 + nrm(ks[10], (DEPTH, HEAD_DIM), 0.02),
        "qg_b": 1.0 + nrm(ks[11], (DEPTH, HEAD_DIM), 0.02),
        "kg_b": 1.0 + nrm(ks[12], (DEPTH, HEAD_DIM), 0.02),
        "sink_b": nrm(ks[13], (DEPTH, N_HEADS_B), 0.5),
        "conv_w": nrm(ks[14], (DEPTH, CONV_K, BRANCH_WIDTH), CONV_K ** -0.5),
        "w_branch": nrm(ks[15], (DEPTH, N_BRANCH, BRANCH_WIDTH, D), BRANCH_WIDTH ** -0.5),
        "w_out": nrm(ks[16], (DEPTH, D, D), D ** -0.5),
        "w_router": nrm(ks[17], (DEPTH, D, N_EXPERTS), D ** -0.5),
        "w_e_gate": nrm(ks[18], (DEPTH, N_EXPERTS, D, EXPERT_HIDDEN), D ** -0.5),
        "w_e_up": nrm(ks[19], (DEPTH, N_EXPERTS, D, EXPERT_HIDDEN), D ** -0.5),
        "w_e_down": nrm(ks[20], (DEPTH, N_EXPERTS, EXPERT_HIDDEN, D), EXPERT_HIDDEN ** -0.5),
    }

def second_block(x, c, ctx, c_ctx, w_ada, b_ada, g_mix, g_ffn, w_in, qg_a, kg_a, qg_b, kg_b, sink_b,
              conv_w, w_branch, w_out, w_router, w_e_gate, w_e_up, w_e_down):
    n = x.shape[1]
    rope = rope_tables(n)
    silu_c = jax.nn.silu(c)
    silu_cc = jax.nn.silu(c_ctx)
    xc = ctx
    for l in range(DEPTH):
        last = l == DEPTH - 1
        mod = silu_c @ w_ada[l] + b_ada[l]
        sh1, sc1, gt1, sh2, sc2, gt2 = [m[:, None, :] for m in jnp.split(mod, 6, axis=-1)]
        modc = silu_cc @ w_ada[l] + b_ada[l]
        shc1, scc1, gtc1, shc2, scc2, gtc2 = jnp.split(modc, 6)

        hc = modulate(rmsnorm(xc, g_mix[l]), shc1, scc1)
        pc = hc @ (w_in[l][:, :KV_END] if last else w_in[l])
        ctx_kv = kv_heads(pc[..., :KV_END], kg_a[l], kg_b[l], None)

        h = modulate(rmsnorm(x, g_mix[l]), sh1, sc1)
        p = h @ w_in[l]
        x = x + gt1 * latent_mixer(p, ctx_kv, rope, qg_a[l], kg_a[l], qg_b[l], kg_b[l], sink_b[l],
                                   conv_w[l], w_branch[l], w_out[l])
        h2 = modulate(rmsnorm(x, g_ffn[l]), sh2, sc2)
        x = x + gt2 * expert_choice_ffn(h2, w_router[l], w_e_gate[l], w_e_up[l], w_e_down[l])

        if not last:
            xc = xc + gtc1 * context_mixer(pc, ctx_kv, qg_a[l], qg_b[l], sink_b[l], conv_w[l],
                                           w_branch[l], w_out[l])
            hc2 = modulate(rmsnorm(xc, g_ffn[l]), shc2, scc2)
            xc = xc + gtc2 * expert_choice_ffn(hc2, w_router[l], w_e_gate[l], w_e_up[l], w_e_down[l])
    return x


def setup_inputs(seed=0):
    out = dict(first_inputs(seed))
    for name, value in second_inputs(seed + 1).items():
        if name != "x":
            out[name + "_2"] = value
    return out


def reference(
    x, c, positions, w_ada, b_ada, g_norm1, w_in, b_in, g_q_lat, w_uq, g_kv_lat, w_ukv,
    g_q_head, g_k_head, w_branch_mla, w_branch_sb, w_out, g_norm2, w_up, w_conv, b_conv, w_down,
    c_2, ctx_2, c_ctx_2, w_ada_2, b_ada_2, g_mix_2, g_ffn_2, w_in_2, qg_a_2, kg_a_2, qg_b_2,
    kg_b_2, sink_b_2, conv_w_2, w_branch_2, w_out_2, w_router_2, w_e_gate_2, w_e_up_2,
    w_e_down_2,
):
    x = first_block(
        x, c, positions, w_ada, b_ada, g_norm1, w_in, b_in, g_q_lat, w_uq, g_kv_lat, w_ukv,
        g_q_head, g_k_head, w_branch_mla, w_branch_sb, w_out, g_norm2, w_up, w_conv, b_conv,
        w_down,
    )
    return second_block(
        x, c_2, ctx_2, c_ctx_2, w_ada_2, b_ada_2, g_mix_2, g_ffn_2, w_in_2, qg_a_2, kg_a_2,
        qg_b_2, kg_b_2, sink_b_2, conv_w_2, w_branch_2, w_out_2, w_router_2, w_e_gate_2,
        w_e_up_2, w_e_down_2,
    )


_drawn_inputs = setup_inputs


def setup_inputs(seed=0):
    import zlib

    import numpy as np

    out = dict(_drawn_inputs(seed))
    spreads = {}
    factors = {'g_norm1': 7.918,
     'b_in': 6.365,
     'g_q_lat': 8.0,
     'g_kv_lat': 8.0,
     'g_q_head': 8.0,
     'g_k_head': 8.0,
     'g_norm2': 5.15,
     'b_conv': 5.183,
     'ctx_2': 2.939,
     'g_mix_2': 5.053,
     'g_ffn_2': 17.013,
     'qg_a_2': 38.721,
     'kg_a_2': 37.868,
     'qg_b_2': 50.464,
     'kg_b_2': 58.255,
     'sink_b_2': 8.0}
    for name, (base, spread) in spreads.items():
        noise = np.random.default_rng([zlib.crc32(name.encode()), seed]).standard_normal(out[name].shape)
        drawn = base * np.exp(spread * noise) if base else spread * noise
        out[name] = __import__('jax').numpy.asarray(drawn.astype(out[name].dtype))
    for name, factor in factors.items():
        out[name] = (out[name] * factor).astype(out[name].dtype)
    return out
```

```python
from contextlib import ExitStack

import numpy as np

import concourse.bass as bass
from concourse import mybir

F32 = mybir.dt.float32
I32 = mybir.dt.int32
U32 = mybir.dt.uint32
ALU = mybir.AluOpType
ACT = mybir.ActivationFunctionType
AX = mybir.AxisListType.X

P = 128
T = 256
D = 1024
KT = D // P
SLOTS = 6
CH = 4096
EPS = 1e-6
FF = 2816
FT = FF // P
H1 = 4
SC_MLA = 192 ** -0.5
SC_SB = 128 ** -0.5
HB = 8
SC_B = 64 ** -0.5
E = 16
CAP = 32
PAIRS = E // 2
BIG = -1e30

TRIPS = {"a0": 1, "b1": 2, "d0": 1, "e0": PAIRS, "d1": 1, "e1": PAIRS}
PHASES = ["a0", "b1", "d0", "e0", "d1", "e1"]


def each(name, n):
    return [(name, i) for i in range(n)]


def plan_ada():
    out = [("ada_part", 0)]
    for i in range(1, 12):
        out += [("ada_part", i), ("ada_col", i - 1)]
    return out + [("ada_col", 11)]


def ada_at(phase, site, t):
    if phase != "d0":
        return []
    if site == "cx":
        return [("ada_col", 3 + t), ("ada_part", 4 + t)]
    if site == "b":
        return [("ada_part", t // 2)] if t % 2 else [("ada_col", t // 2 - 1)] if t else []
    if site == "c":
        return [("ada_col", 7)] if t == 0 else []
    return {"a": [], "norm": each("ada_part", 12)[8:10],
            "logit": each("ada_col", 12)[8:10] + each("ada_part", 12)[10:], "htok": each("ada_col", 12)[10:]}[site]


def plan_up():
    out = []
    for c in range(11):
        out += [("ada_part", c), ("up", 2 * c), ("ada_col", c), ("up", 2 * c + 1)]
    return out + [("ada_part", 11)] + [("down", t) for t in range(4)] + [("ada_col", 11)] + [("down", t) for t in range(4, 8)]


def plan_heads(n, scores, turn, value, early=(), before=(), after=()):
    out = list(scores(0)) + list(scores(1)) + list(early)
    for h in range(n):
        out += list(before if h == n - 1 else ()) + turn(h) + list(after if h == n - 1 else ())
        if h + 2 < n:
            out += scores(h + 2)
        out += value(h)
    return out


def mla_heads():
    return plan_heads(H1, lambda h: [("s", 2 * h), ("s", 2 * h + 1)], lambda h: [("turn", h)],
                      lambda h: [("mla_v", h)], early=[("gates", 0)], before=[("gates", 1)])


def units(layer):
    return [(s, h) for s in range(2 if layer == 0 else 1) for h in range(HB)]


def gqa_heads(layer, b):
    n = len(units(layer))
    return plan_heads(n, lambda u: [("s" + b, 2 * u), ("s" + b, 2 * u + 1)],
                      lambda u: [("turn" + b, 2 * u), ("turn" + b, 2 * u + 1)],
                      lambda u: [("val" + b, u // 2)] if u % 2 else [],
                      before=[("gate" + b, 0)], after=[("gate" + b, 1)])


NORMED = each("kk", 2) + each("qa", 4) + each("qb", 4)


def norm_jobs():
    out = []
    for n in range(len(NORMED) + 2):
        if 4 <= n < 6:
            out.append(("khalf", n - 4))
        if n < len(NORMED):
            out.append(NORMED[n])
        if n == 1:
            out += each("vv", 2)
        if 0 <= n - 1 < len(NORMED):
            out.append(("ss", n - 1))
        if n >= 2:
            out.append(("swap", n - 2))
    return out


def branch_jobs(b, phase):
    return [x for t in range(KT) for x in ([("gate" + b, t)] if b == "c" or t >= 2 else []) + [("br" + b, t)] + ada_at(phase, b, t)]


def plan(phase):
    if phase == "a0":
        return plan_ada()
    if phase == "b1":
        out = [("ss1", 0)] + each("lat", 4) + each("qsb", 4) + [("sslat", 0)] + each("ksb", 4) + each("z", 4)
        out += each("q", 6) + each("k", 4) + each("vmla", 2) + each("ssq", 3) + each("ssk", 3) + each("vsb", 2)
        out += each("cum", 4) + [("swap", 0), ("swap", 1)] + each("sb_v", 4)
        out += mla_heads()
        out += [("br", 0), ("br", 1)] + [x for t in range(2, KT) for x in (("gates", t), ("br", t))]
        out += each("out", KT) + [("ss2", 0)] + plan_up()
    elif phase in ("d0", "d1"):
        layer = int(phase[1])
        out = [("ss1", 0)] + norm_jobs()
        for b in "ab":
            out += gqa_heads(layer, b) + branch_jobs(b, phase)
        out += [x for t in range(4) for x in [("cc", t), ("cx", t), ("cb", t)] + ada_at(phase, "cx", t)]
        out += branch_jobs("c", phase) + each("out", KT) + [("ss2", 0)] + ada_at(phase, "norm", 0)
        out += [("logit", 0)] + ada_at(phase, "logit", 0) + [("afft", 0)] + each("htok", 4 if layer else 8)
        out += ada_at(phase, "htok", 0)
        out += [("cols", 0), ("pick", 0)] + each("xs", 2)
    else:
        out = [x for e in range(2) for x in (("eg", e), ("eu", e))] + [x for e in range(2) for x in (("eh", e), ("ey", e))]
        out += [("pick", 0)] + each("scat", KT) + each("xs", 2)
    return out + each("pad", -len(out) % 8)


def plan_chunks(phase):
    if phase == "a0":
        return each("ada", 12)
    if phase == "b1":
        out = [("lat", 0), ("qsb", 0), ("ksb", 0), ("low", 0), ("vsb", 0), ("gm", 0), ("gs", 0), ("wm", 0), ("ws", 0),
               ("gm", 1), ("gs", 1), ("out", 0), ("out", 1)]
        return out + [x for c in range(11) for x in (("ada", c), ("up", c))] + [("ada", 11)] + each("down", 6)
    if phase[0] == "d":
        def ada(site, ts):
            return [("ada", i) for t in ts for job, i in ada_at(phase, site, t) if job == "ada_part"]

        out = [("kv", 0), ("qa", 0), ("qb", 0)]
        for b in "ab":
            out += [("gate" + b, 0), ("w" + b, 0)] + ada(b, range(4)) + [("gate" + b, 1)] + ada(b, range(4, 8))
        out += [("conv", 0)] + ada("cx", [0]) + [("conv", 1)] + ada("cx", [1]) + [("conv", 2)] + ada("cx", [2, 3])
        out += [("gatec", 0), ("wc", 0), ("gatec", 1)]
        return out + each("out", 2) + ada("norm", [0]) + [("router", 0)] + ada("logit", [0])
    return [("gu", i) for i in range(8)] + each("dn", 4)


CHUNK_PLANS = {ph: plan_chunks(ph) for ph in PHASES}
CHUNKS = {ph: len(CHUNK_PLANS[ph]) for ph in PHASES}
assert all(n % SLOTS == 0 for n in CHUNKS.values()), CHUNKS
PLANS = {ph: plan(ph) for ph in PHASES}
NUMBER = {ph: {x: j for j, x in enumerate(PLANS[ph])} for ph in PHASES}

CONST = {}
ROUND = 12582912.0
TWO_PI = (6.28125, 0.0019350051879882812, 3.019916e-07)

PER = {
    "b1": {
        "sq_ready": 4, "root_ready": 5, "h_ready": 16, "act_step": 12, "log_ready": 1, "sb_ready": 4,
        "probs_ready": 8, "conv_ready": 22, "gate_ready": 22, "h_scaled": 16, "dve_step": 76,
        "softplus_ready": 1, "lat_ready": 1, "q_scaled": 1, "k_scaled": 1, "q_ready": 1, "k_ready": 1,
        "top_ready": 8, "probs_normed": 8, "merged_ready": 8, "hid_ready": 22,
    },
    "e0": {
        "egate_ready": 2, "onehot_ready": 1, "picked_ready": 1,
    },
    "e1": {
        "egate_ready": 2, "onehot_ready": 1, "picked_ready": 1,
    },
}


def constants():
    parts = []

    def put(name, a):
        CONST[name] = (sum(x.shape[1] for x in parts), a.shape[1])
        parts.append(a.astype(np.float32))

    i = np.arange(P)
    row, col = i[:, None], i[None, :]
    put("ident", np.concatenate([row == col, row == col[:, :64]], 1))
    put("ones", np.ones((P, P)))
    put("colhalf", (np.arange(192)[None, :] // 64 != 1) * np.ones((P, 1)))
    put("rowhalf", np.concatenate([(row // 64 == j) * np.ones((1, P)) for j in range(2)], 1))
    put("block64", row // 64 == col // 64)
    put("swap32", (row ^ 32) == col)
    put("tri", row >= col)
    put("causal", np.concatenate([np.zeros((P, P)), np.where(col <= row, 0.0, BIG)], 1))
    past = np.where(row < col, 0.0, BIG)
    put("past", np.concatenate([past, np.zeros((P, P)), past], 1))
    put("sumsel", (row % 32 == np.arange(2)[None, :]))
    freq = np.float32(1.0) / (np.float32(10000.0) ** (np.arange(32, dtype=np.float32) * np.float32(2.0 / 64)))
    put("freq", np.tile(freq, 4)[:, None])
    put("sign", np.tile(np.repeat([-1.0, 1.0], 32), 2)[:, None])
    put("ctxrow", (row // 16 == 1) * 256.0)
    keys = np.arange(T)[None, :]
    put("window", np.concatenate([np.where(abs(row + P * t - keys) <= 128, 0.0, BIG) for t in range(2)], 1))
    put("iota", np.arange(2 * T)[None, :] * np.ones((P, 1)))
    t = np.arange(T)
    inv = (np.float32(10000.0) ** (-np.arange(16, dtype=np.float32) / np.float32(16))).astype(np.float32)
    ang = np.concatenate([(t // 64).astype(np.float32)[:, None] * inv, (t % 64).astype(np.float32)[:, None] * inv], 1)
    c, s = np.cos(ang), np.sin(ang)
    put("cos", np.tile(c.T, (4, 1)))
    put("sin", np.concatenate([-s.T, s.T, -s.T, s.T], 0))
    return np.ascontiguousarray(np.concatenate(parts, 1))


constants()
NC_COLS = sum(w for _, w in CONST.values())
NC_FIRST = CONST["window"][0]


def layout(fields):
    at, out = 0, {}
    for name, w in fields:
        out[name] = (at, w)
        at += w
    return out, at


PAR1, N1 = layout([("b_ada", 48), ("g1", 8), ("b_lat", 4), ("b_qsb", 4), ("b_ksb", 4), ("b_gm", 8), ("b_gs", 8),
                   ("g_qlat", 2), ("g_kvlat", 1), ("gq", 2), ("gk", 2), ("g2", 8), ("cw", 3 * 2 * FT),
                   ("cb", 2 * FT)])
PAR2, N2 = layout([("b_ada", 48), ("g1", 8), ("g2", 8), ("gqa", 1), ("gqb", 1), ("gk", 2), ("sink", 8), ("cw", 12)])


class Book:

    def __init__(self, nc, ctx, per):
        self.nc, self.ctx, self.per = nc, ctx, per
        self.signals, self.engine, self.loop, self.seen, self.totals = [], None, None, {}, {}

    def semaphore(self, name):
        s = Signal(self, name)
        self.signals.append(s)
        return s

    def start(self, engine):
        if self.engine:
            self.totals[self.engine] = {s.name: (s.base + s.taken, s.all) for s in self.signals}
        self.engine, self.loop = engine, None
        for s in self.signals:
            s.base = s.taken = s.made = s.all = 0

    def enter(self, name, reg):
        self.loop = (name, reg)
        for s in self.signals:
            s.base, s.taken, s.made = s.base + s.taken, 0, 0

    def leave(self, name, trips):
        for s in self.signals:
            n = self.per.get((name, s.name), 0)
            assert not self.per or s.taken in (0, n), (self.engine, name, s.name, s.taken, n)
            if s.made:
                self.seen[name, s.name] = s.made
            s.base, s.taken, s.made = s.base + trips * n, 0, 0
        self.loop = None


class Signal:

    def __init__(self, book, name):
        self.book, self.name = book, name
        self.sem = book.ctx.enter_context(book.nc.semaphore(name))
        self.base = self.taken = self.made = self.all = 0

    def inc(self):
        self.made += 1
        self.all += 1 if not self.book.loop else TRIPS[self.book.loop[0]]
        return self.sem, 1

    def take(self, n=1):
        self.taken += n
        if self.book.loop:
            name, reg = self.book.loop
            return self.sem, reg * self.book.per.get((name, self.name), 1) + (self.base + self.taken)
        return self.sem, self.base + self.taken

    def skip(self, n=1):
        self.taken += n


class Rings:

    def __init__(self, nc, ctx):
        self.banks = [ctx.enter_context(nc.psum_tensor(f"bank{b}", [P, 512], F32)) for b in range(8)]
        self.full_sem = [ctx.enter_context(nc.semaphore(f"bank{b}_full")) for b in range(8)]
        self.free_sem = [ctx.enter_context(nc.semaphore(f"bank{b}_free")) for b in range(8)]
        self.slot_full = [ctx.enter_context(nc.semaphore(f"slot{s}_full")) for s in range(SLOTS)]
        self.slot_used = [ctx.enter_context(nc.semaphore(f"slot{s}_used")) for s in range(SLOTS)]

    def phase(self, name, reg=0):
        self.name, self.reg = name, reg
        self.job0 = self.chunk0 = 0
        for ph in PHASES[:PHASES.index(name)]:
            self.job0 += TRIPS[ph] * len(PLANS[ph]) // 8
            self.chunk0 += TRIPS[ph] * CHUNKS[ph] // SLOTS

    def use(self, job, i):
        j = NUMBER[self.name][job, i]
        return j % 8, self.reg * (len(PLANS[self.name]) // 8) + (self.job0 + j // 8 + 1)

    def bank(self, job, i=0):
        return self.banks[NUMBER[self.name][job, i] % 8]

    def full(self, job, i=0):
        b, n = self.use(job, i)
        return self.full_sem[b], n

    def free(self, job, i=0):
        b, n = self.use(job, i)
        return self.free_sem[b], n

    def filled(self, job, i=0):
        return self.full_sem[NUMBER[self.name][job, i] % 8], 1

    def freed(self, job, i=0):
        return self.free_sem[NUMBER[self.name][job, i] % 8], 1

    def chunk(self, name, i=0):
        return CHUNK_PLANS[self.name].index((name, i))

    def loaded(self, c):
        return self.slot_full[c % SLOTS], self.reg * (16 * (CHUNKS[self.name] // SLOTS)) + 16 * (self.chunk0 + c // SLOTS + 1)

    def evac(self, job, i=0):
        b, n = self.use(job, i)
        return self.free_sem[b], n + 1


def two_stacks(nc, weights, const, par1, par2, c_cols, x_cols, positions, out, per):
    ctx = ExitStack()
    with ctx:
        def sb(name, shape, dt=F32):
            return ctx.enter_context(nc.sbuf_tensor(name, shape, dt))

        book = Book(nc, ctx, per)
        R = Rings(nc, ctx)
        ring = sb("ring", [P, SLOTS, CH])
        cst = sb("cst", [P, NC_COLS])
        pars1 = sb("pars1", [P, 2, N1])
        pars2 = sb("pars2", [P, 2, N2])
        p1 = sb("p1", [P, N1])
        silc = sb("silc", [P, 2, KT, 2])
        cact = sb("cact", [P, KT, 32])
        mod_next = sb("mod_next", [P, 48, 2])
        mod = sb("mod", [P, 48, 2])
        gains = sb("gains", [P, KT, 2])
        small = sb("small", [P, 24])
        X = sb("X", [P, KT, 2 * T])
        h = sb("h", [P, KT, 2 * T])
        WORK = 15360
        work = sb("work", [P, WORK])

        def const_of(name, j=0, w=None):
            at, width = CONST[name]
            w = w or width
            return cst[:, at + j * w:at + (j + 1) * w]

        ident, ones, block64 = const_of("ident", 0, P), const_of("ones"), const_of("block64")
        swap32, swap64, tri = const_of("swap32"), const_of("ident")[:, 64:192], const_of("tri")
        colhalf = [const_of("colhalf")[:, 64 * j:64 * j + P] for j in range(2)]

        def slots_of(a, s):
            return a.rearrange("p (e r) -> p e r", r=64)[:, :, 32 * s:32 * s + 32]

        def q1(name, j=0, w=1):
            at, _ = PAR1[name]
            return p1[:, at + j:at + j + w]

        def q2(layer, name, j=0, w=1):
            at, _ = PAR2[name]
            return pars2[:, layer, at + j:at + j + w]

        def area(at, *shape):
            n = int(np.prod(shape))
            assert at + n <= WORK, (at, shape)
            a = work[:, at:at + n]
            if len(shape) == 2:
                a = a.rearrange("p (a b) -> p a b", a=shape[0])
            if len(shape) == 3:
                a = a.rearrange("p (a b c) -> p a b c", a=shape[0], b=shape[1])
            return a

        qf, kf = area(0, 6, T), area(1536, 6, T)
        sq = area(3072, 11, T)
        ms, rs = area(5888, 6, T), area(7424, 6, T)
        sp = area(8960, H1, 384)
        zm = area(10496, H1, 384)
        qsb, ksb = area(12032, H1, T), area(13056, H1, T)
        vmla = area(14080, 2, 512)
        krw, lat = h[:, 0, T:2 * T], h[:, 1:4, T:2 * T]
        latsq = h[:, 4:7, T:2 * T]
        vsb = X[:, 0:4, T:2 * T]
        ysb, ymla = X[:, 4:8, T:2 * T], area(3072, H1, T)
        sc1 = area(4096, 4, T)
        pt1 = area(5120, 2, 384)
        merged1 = area(8960, KT, T)
        sig1, tmp1 = area(11008, 2, 512), area(12032, 2, 512)
        hid = area(0, FT, T)
        conv1, sg1 = area(5632, 3, 512), area(7168, 2, T)
        apart = area(14080, 2, 512)
        room = cst[:, NC_FIRST:NC_FIRST + 1536]
        trig = room[:, 0:512].rearrange("p (a b) -> p a b", a=2)

        kf2, kg2 = area(0, 2, 512), area(1024, 2, 512)
        vt2 = area(2048, 4, 256)
        qf2 = area(3072, 4, 512)
        y2 = area(5120, 4, 512)
        merged2 = area(7168, KT, 512)
        sq2 = area(11264, 4, 512)
        ms2, rs2 = area(13312, 2, 512), area(14336, 2, 512)
        pr2 = area(11264, 4, 512)
        pt2 = area(13312, 2, 1024)
        sig2, tmp2 = area(11264, 2, 512), area(12288, 2, 512)
        xs2c, uc, tc = area(11264, 2, 512), area(12288, 2, 512), area(13312, 2, 512)
        apart2 = area(14336, 2, 512)
        qb2 = merged2[:, 4:8]
        raw2 = [kf2[:, 0], kf2[:, 1]] + [f[:, j] for f in (qf2, qb2) for j in range(4)]
        rtmp = area(5120, T)
        htok = area(0, 4, D)
        wk, vals, seli = area(4096, T), area(4352, 64), area(4416, 64)
        aff = area(4480, 2, 32)
        lg = area(4544, 4, 16)
        eidx = sb("eidx", [P, CAP], U32)
        idxc, gatec = area(4608, PAIRS + 1), area(4617, PAIRS)
        oh, og = area(4632, 512), area(5144, 512)
        pk = area(5656, 4, P)
        xs = area(6168, KT, P)
        sge, ae = area(7192, 2, 512), area(8216, 2, 512)
        hte = area(9240, 2, 512)
        ye = area(10264, D)

        names = ("sq_ready", "root_ready", "h_scaled", "h_ready", "act_step", "dve_step", "log_ready",
                 "softplus_ready", "lat_ready", "q_scaled", "k_scaled", "sb_ready", "q_ready", "k_ready", "top_ready",
                 "probs_ready", "probs_normed", "merged_ready", "conv_ready", "gate_ready", "hid_ready", "c_ready", "c_done",
                 "angle_ready", "onehot_ready", "picked_ready", "egate_ready", "logits_ready", "affinities_ready",
                 "slots_ready", "qb_moved")
        (sq_ready, root_ready, h_scaled, h_ready, act_step, dve_step, log_ready, softplus_ready,
         lat_ready, q_scaled, k_scaled, sb_ready, q_ready, k_ready, top_ready, probs_ready, probs_normed,
         merged_ready, conv_ready, gate_ready, hid_ready, c_ready, c_done, angle_ready, onehot_ready, picked_ready,
         egate_ready, logits_ready, affinities_ready, slots_ready, qb_moved) = [book.semaphore(n) for n in names]
        c_in, const_in, par_in, x_in, second_in, pos_in, out_done = [ctx.enter_context(nc.semaphore(n)) for n in (
            "c_in", "const_in", "par_in", "x_in", "second_in", "pos_in", "out_done")]
        vrow = room[0:1, 512:1536].rearrange("p (a b) -> p a b", a=2)
        posi = area(1280, T).bitcast(I32)
        craw, csig = area(1536, 32), area(1568, 32)
        ang = area(0, 5, T)
        block = ctx.enter_context(nc.Block())

        @block.sync
        def _(sp_):
            book.start("SP")
            sp_.dma_start(craw[:, :], c_cols).then_inc(c_in, 16)
            sp_.dma_start(cst[:, 0:NC_FIRST], const[:, 0:NC_FIRST]).then_inc(const_in, 16)
            for s in range(SLOTS):
                sp_.dma_start(ring[:, s, :], weights[s]).then_inc(R.slot_full[s], 16)
                if s == 2:
                    sp_.dma_start(pars1[:, :, :], par1[:, :, 0:N1]).then_inc(par_in, 16)
                    sp_.dma_start(vrow[:, :, :], par1[0:1, :, N1:N1 + 512]).then_inc(par_in, 16)
                if s == 4:
                    sp_.dma_start(X[:, :, 0:T], x_cols[:, 0]).then_inc(x_in, 16)
            rounds = weights.shape[0] // SLOTS
            with sp_.Fori(1, rounds) as i:
                for s in range(SLOTS):
                    sp_.wait_ge(R.slot_used[s], i)
                    sp_.dma_start(ring[:, s, :], weights[bass.ds(i * SLOTS + s, 1)].rearrange("a p c -> (a p) c"))\
                       .then_inc(R.slot_full[s], 16)
            R.phase("e1", PAIRS - 1)
            sp_.wait_ge(*R.evac("scat", KT - 1))
            sp_.dma_start(out, X[:, :, 0:T]).then_inc(out_done, 16)
            sp_.wait_ge(out_done, 16)

        @block.gpsimd
        def _(pool):
            pool.dma_start(posi[:, :], positions.partition_broadcast(P)).then_inc(pos_in, 16)
            pool.dma_start(pars2[:, :, :], par2).then_inc(second_in, 16)
            R.phase("b1", 1)
            pool.wait_ge(*R.evac("br", KT - 1))
            pool.dma_start(X[:, :, T:2 * T], x_cols[:, 1]).then_inc(second_in, 16)
            pool.dma_start(cst[:, NC_FIRST:NC_COLS], const[:, NC_FIRST:NC_COLS]).then_inc(second_in, 16)

        @block.tensor
        def _(pe):
            book.start("PE")
            used = []

            def mm(o, l, r, start, stop, signal=None, turn=False):
                ins = nc.tensor.matmul(o, l, r, start=start, stop=stop, is_transpose=True) if turn else \
                    nc.tensor.matmul(o, l, r, start=start, stop=stop)
                if signal is not None:
                    ins.then_inc(*signal)
                elif used:
                    ins.then_inc(R.slot_used[used.pop(0) % SLOTS], 1)

            def product(job, i, groups):
                pe.wait_ge(*R.free(job, i))
                last = len(groups) - 1
                for g, (cols, terms) in enumerate(groups):
                    for n, (l, r) in enumerate(terms):
                        end = n == len(terms) - 1
                        mm(cols, l, r, n == 0, end, R.filled(job, i) if end and g == last else None)

            def turned(job, i, pieces):
                pe.wait_ge(*R.free(job, i))
                for n, (cols, src) in enumerate(pieces):
                    k = src.shape[0]
                    mm(cols, src, ident[0:k, 0:k], True, True,
                       R.filled(job, i) if n == len(pieces) - 1 else None, turn=True)

            def tile_of(c, k, j, w=512):
                return ring[:, c % SLOTS, k * w + j * P:k * w + (j + 1) * P]

            def ada(jobs, part):
                for job, i in jobs:
                    bank = R.bank(job, i)
                    if job == "ada_col":
                        pe.wait_ge(*R.evac("ada_part", i))
                        product(job, i, [(bank[:, 2 * j:2 * j + 2], [(part[:, i % 2, j * P:(j + 1) * P],
                                                                      const_of("sumsel"))]) for j in range(4)])
                        continue
                    c = R.chunk("ada", i)
                    pe.wait_ge(*R.loaded(c))
                    pe.wait_ge(*R.free(job, i))
                    for k in range(KT):
                        g = 32 * (k % 4)
                        mm(bank[g:g + 32, :], cact[:, k, :], ring[:, c % SLOTS, k * 512:(k + 1) * 512],
                           k < 4, k >= 4, R.filled(job, i) if k == KT - 1 else None)
                    used.append(c)

            def sumsq(job, nt):
                pe.wait_ge(*R.free(job))
                bank = R.bank(job)
                for k in range(KT):
                    if k % 4 == 0:
                        pe.wait_ge(*sq_ready.take())
                    mm(bank[:, 0:nt], ones, h[:, k, 0:nt], k == 0, k == KT - 1, R.filled(job) if k == KT - 1 else None)

            def from_h(job, i, c, j, nt, streams=0):
                pe.wait_ge(*R.free(job, i))
                bank = R.bank(job, i)
                for k in range(KT):
                    if streams:
                        pe.wait_ge(*h_ready.take(streams))
                    mm(bank[:, 0:nt], tile_of(c, k, j), h[:, k, 0:nt], k == 0, k == KT - 1,
                       R.filled(job, i) if k == KT - 1 else None)

            def first_stack(L):
                sumsq("ss1", T)
                pe.wait_ge(*R.loaded(R.chunk("lat")))
                for j in range(4):
                    from_h("lat", j, R.chunk("lat"), j, T, 1 if j == 0 else 0)
                used.append(R.chunk("lat"))
                low, vs = R.chunk("low"), R.chunk("vsb")
                for job in ("qsb", "ksb"):
                    c = R.chunk(job)
                    pe.wait_ge(*R.loaded(c))
                    for j in range(4):
                        from_h(job, j, c, j, T)
                    used.append(c)
                    if job == "qsb":
                        bank = R.bank("sslat")
                        pe.wait_ge(*R.evac("lat", 3))
                        product("sslat", 0, [(bank[:, 0:T], [(ones, latsq[:, 0]), (ones, latsq[:, 1])]),
                                             (bank[:, T:512], [(ones, latsq[:, 2])])])
                for i in range(H1):
                    if i == 0:
                        pe.wait_ge(*R.evac("ksb", 3))
                    product("z", i, [(R.bank("z", i)[:, 0:T], [(ksb[:, i, 0:P], qsb[:, i, :])]),
                                     (R.bank("z", i)[:, T:384], [(ksb[:, i, P:T], qsb[:, i, P:T])])])
                pe.wait_ge(*R.loaded(low))
                pe.wait_ge(*lat_ready.take())
                base = ring[:, low % SLOTS, :]
                for j in range(6):
                    product("q", j, [(R.bank("q", j)[:, 0:T], [(base[:, k * 768 + j * P:k * 768 + (j + 1) * P],
                                                                lat[:, k]) for k in range(2)])])
                for j in range(4):
                    product("k", j, [(R.bank("k", j)[:, 0:T], [(base[:, 1536 + j * P:1536 + (j + 1) * P], lat[:, 2])])])
                for i in range(2):
                    product("vmla", i, [(R.bank("vmla", i)[:, :], [(lat[:, 2, i * P:(i + 1) * P],
                                                                    base[:, 2048:2560])])])
                used.append(low)

                def head_squares(job, s0, rope):
                    for m in range(2):
                        bank = R.bank(job, m)
                        product(job, m, [(bank[:, j * T:(j + 1) * T], [(ones, sq[:, s0 + 2 * m + j]), (const_of("rowhalf", j, P), sq[:, rope[m]])])
                                         for j in range(2)])
                    bank = R.bank(job, 2)
                    product(job, 2, [(bank[:, m * T:(m + 1) * T], [(colhalf[0], sq[:, s0 + 2 * m]),
                                                                   (colhalf[1], sq[:, s0 + 2 * m + 1]),
                                                                   (block64, sq[:, rope[m]])]) for m in range(2)])

                pe.wait_ge(*R.evac("q", 5))
                head_squares("ssq", 0, (4, 5))
                pe.wait_ge(*R.evac("k", 3))
                head_squares("ssk", 6, (10, 10))
                pe.wait_ge(*R.loaded(vs))
                for i in range(2):
                    terms = [(h[:, k, i * P:(i + 1) * P], ring[:, vs % SLOTS, k * 512:(k + 1) * 512]) for k in range(KT)]
                    terms.append((ones[0:1, :], vrow[:, bass.ds(L, 1), :].rearrange("p a n -> p (a n)")))
                    product("vsb", i, [(R.bank("vsb", i)[:, :], terms)])
                used.append(vs)
                pe.wait_ge(*softplus_ready.take())
                for i in range(H1):
                    bank = R.bank("cum", i)
                    pe.wait_ge(*R.free("cum", i))
                    mm(bank[:, 0:T], tri, sp[:, i, 0:T], True, False)
                    mm(bank[:, P:T], ones, sp[:, i, T:384], False, True)
                    mm(bank[:, T:384], tri, sp[:, i, T:384], True, True, R.filled("cum", i))
                for n, (scaled, f) in enumerate(((q_scaled, qf), (k_scaled, kf))):
                    pe.wait_ge(*scaled.take())
                    product("swap", n, [(R.bank("swap", n)[:, :].rearrange("p (a b) -> p a b", a=2), [(swap32, f[:, 4:6])])])
                for i in range(H1):
                    pe.wait_ge(*sb_ready.take())
                    bank = R.bank("sb_v", i)
                    if i == 0:
                        pe.wait_ge(*R.evac("vsb", 1))
                    pe.wait_ge(*R.free("sb_v", i))
                    v0, v1 = (X[:, 2 * t + i // 2, T + (i % 2) * P:T + (i % 2) * P + P] for t in range(2))
                    mm(bank[:, 0:T], v0, sp[:, i, 0:T], True, False)
                    mm(bank[:, P:T], v1, sp[:, i, T:384], False, True, R.filled("sb_v", i))
                def both_gates(t):
                    cm, cs = R.chunk("gm", t // 4), R.chunk("gs", t // 4)
                    if t % 4 == 0:
                        pe.wait_ge(*R.loaded(cm))
                        pe.wait_ge(*R.loaded(cs))
                    bank = R.bank("gates", t)
                    product("gates", t, [(bank[:, n * T:(n + 1) * T], [(tile_of(c, k, t % 4), h[:, k, 0:T]) for k in range(KT)])
                                         for n, c in enumerate((cm, cs))])
                    if t % 4 == 3:
                        used.extend((cm, cs))

                for job, i in mla_heads():
                    if job == "gates":
                        both_gates(i)
                    elif job == "s":
                        hd, qt = divmod(i, 2)
                        n = (qt + 1) * P
                        if i == 0:
                            pe.wait_ge(*q_ready.take())
                            pe.wait_ge(*k_ready.take())
                        r0 = 64 * (hd % 2)
                        product("s", i, [(R.bank("s", i)[:, 0:n], [
                            (qf[:, hd, qt * P:(qt + 1) * P], kf[:, hd, 0:n]),
                            (qf[r0:r0 + 64, 4 + hd // 2, qt * P:(qt + 1) * P], kf[r0:r0 + 64, 4 + hd // 2, 0:n])])])
                    elif job == "turn":
                        pe.wait_ge(*probs_normed.take(2))
                        bank, a, b = R.bank("turn", i), sc1[:, 2 * i % 4], sc1[:, (2 * i + 1) % 4]
                        turned("turn", i, [(bank[:, 0:P], a[:, 0:P]), (bank[:, P:T], b[:, 0:P]), (bank[:, T:384], b[:, P:T])])
                    else:
                        pe.wait_ge(*R.evac("turn", i))
                        pe.wait_ge(*R.free("mla_v", i))
                        bank = R.bank("mla_v", i)
                        mm(bank[:, 0:T], vmla[:, 0, i * P:(i + 1) * P], pt1[:, i % 2, 0:T], True, False)
                        mm(bank[:, P:T], vmla[:, 1, i * P:(i + 1) * P], pt1[:, i % 2, T:384], False, True,
                           R.filled("mla_v", i))
                pe.wait_ge(*R.evac("sb_v", H1 - 1))
                wm, ws = R.chunk("wm"), R.chunk("ws")
                for t in range(KT):
                    if t >= 2:
                        both_gates(t)
                    if t == 0:
                        pe.wait_ge(*R.loaded(wm))
                        pe.wait_ge(*R.loaded(ws))
                        pe.wait_ge(*R.evac("mla_v", H1 - 1))
                    bank = R.bank("br", t)
                    product("br", t, [(bank[:, n * T:(n + 1) * T], [(tile_of(c, k, t, 1024), y[:, k]) for k in range(4)])
                                      for n, (c, y) in enumerate(((wm, ymla), (ws, ysb)))])
                used.extend((wm, ws))
                out_product(merged1, T)
                sumsq("ss2", T)
                for p in range(FT):
                    c = R.chunk("up", p // 2)
                    ada([("ada_col" if p % 2 else "ada_part", p // 2)], apart)
                    if p % 2 == 0:
                        pe.wait_ge(*R.loaded(c))
                    bank = R.bank("up", p)
                    pe.wait_ge(*R.free("up", p))
                    for half in range(2):
                        for k in range(KT):
                            if p == 0 and half == 0:
                                pe.wait_ge(*h_ready.take())
                            mm(bank[:, half * T:(half + 1) * T], tile_of(c, k, 2 * half + p % 2), h[:, k, 0:T], k == 0,
                               k == KT - 1, R.filled("up", p) if half and k == KT - 1 else None)
                    if p % 2:
                        used.append(c)
                ada([("ada_part", 11)], apart)
                for half in range(2):
                    if half:
                        ada([("ada_col", 11)], apart)
                    for t in range(4):
                        pe.wait_ge(*R.free("down", 4 * half + t))
                    for n in range(3):
                        c = R.chunk("down", 3 * half + n)
                        pe.wait_ge(*R.loaded(c))
                        tiles = range(8 * n, min(8 * n + 8, FT))
                        if half == 0:
                            pe.wait_ge(*hid_ready.take(len(tiles)))
                        for t in range(4):
                            for k in tiles:
                                mm(R.bank("down", 4 * half + t)[:, 0:T], tile_of(c, k - 8 * n, t), hid[:, k],
                                   k == 0, k == FT - 1, R.filled("down", 4 * half + t) if k == FT - 1 else None)
                        used.append(c)
                flush()

            def flush():
                for i in range(8):
                    if ("pad", i) in NUMBER[R.name]:
                        pe.wait_ge(*R.free("pad", i))
                        while used:
                            mm(R.bank("pad", i)[:, 0:1], ones, ones[:, 0:1], True, True)
                        pe.sem_inc(*R.filled("pad", i))
                        pe.sem_inc(*R.freed("pad", i))
                assert not used

            def out_product(merged, nt):
                for t in range(KT):
                    c = R.chunk("out", t // 4)
                    if t % 4 == 0:
                        pe.wait_ge(*R.loaded(c))
                    pe.wait_ge(*R.free("out", t))
                    for k in range(KT):
                        if t == 0:
                            pe.wait_ge(*merged_ready.take())
                        mm(R.bank("out", t)[:, 0:nt], tile_of(c, k, t % 4), merged[:, k, 0:nt], k == 0,
                           k == KT - 1, R.filled("out", t) if k == KT - 1 else None)
                    if t % 4 == 3:
                        used.append(c)

            def dense(layer):
                nt = 2 * T if layer == 0 else T
                sumsq("ss1", 2 * T)
                for job, i in norm_jobs():
                    if job == "kk":
                        kv = R.chunk("kv")
                        if i == 0:
                            pe.wait_ge(*R.loaded(kv))
                        from_h("kk", i, kv, 2 * i, 2 * T, 2 if i == 0 else 0)
                    elif job == "vv":
                        bank = R.bank("vv", i)
                        groups = []
                        for j in range(2):
                            tok = 2 * i + j
                            rhs = [ring[:, kv % SLOTS, k * 512:(k + 1) * 512].rearrange("p (a c n) -> p a c n", a=2, c=2)[:, :, 1]
                                   for k in range(KT)]
                            groups.append((bank[:, j * 256:(j + 1) * 256].rearrange("p (a n) -> p a n", a=2),
                                           [(h[:, k, tok * P:(tok + 1) * P], rhs[k]) for k in range(KT)]))
                        product("vv", i, groups)
                        if i:
                            used.append(kv)
                    elif job in ("qa", "qb"):
                        c = R.chunk(job)
                        if i == 0:
                            pe.wait_ge(*R.loaded(c))
                        from_h(job, i, c, i, nt)
                        if i == 3:
                            used.append(c)
                    elif job == "ss":
                        pe.wait_ge(*R.evac(*NORMED[i]))
                        w = 2 * T if i < 2 else nt
                        product("ss", i, [(R.bank("ss", i)[:, 0:w], [(block64, sq2[:, i % 4, 0:w])])])
                    elif job == "swap":
                        pe.wait_ge(*(k_scaled if i < 2 else q_scaled).take())
                        product("swap", i, [(R.bank("swap", i)[:, 0:T], [(swap32, raw2[i][:, 0:T])])])
                    else:
                        pe.wait_ge(*k_ready.take())
                        product("khalf", i, [(R.bank("khalf", i)[:, :], [(swap64, kf2[:, i])])])
                pe.wait_ge(*R.evac("khalf", 1))
                for n, b in enumerate("ab"):
                    pe.wait_ge(*q_ready.take(4))
                    if b == "b":
                        pe.wait_ge(*qb_moved.take())
                    gqa(layer, n, b)
                    branch(b, nt)
                for n in range(12):
                    t, g = divmod(n, 3)
                    c = R.chunk("conv", n // 4)
                    if n % 4 == 0:
                        pe.wait_ge(*R.loaded(c))
                    from_h(("cc", "cx", "cb")[g], t, c, n % 4, nt)
                    if n % 4 == 3:
                        used.append(c)
                    if g == 2:
                        ada(ada_at(R.name, "cx", t), apart2)
                branch("c", nt)
                out_product(merged2, nt)
                sumsq("ss2", nt)
                ada(ada_at(R.name, "norm", 0), apart2)
                c = R.chunk("router")
                pe.wait_ge(*R.loaded(c))
                pe.wait_ge(*h_ready.take(KT * nt // T))
                bank = R.bank("logit")
                product("logit", 0, [(bank[:, 16 * i:16 * i + 16], [(h[:, k, i * P:(i + 1) * P], ring[:, c % SLOTS, 16 * k:16 * k + 16])
                                                                    for k in range(KT)]) for i in range(nt // P)])
                used.append(c)
                ada(ada_at(R.name, "logit", 0), apart2)
                pe.wait_ge(*affinities_ready.take())
                turned("afft", 0, [(R.bank("afft")[0:32, i * P:(i + 1) * P], aff[:, i]) for i in range(2)])
                for i in range(2 * nt // P):
                    tok, half = divmod(i, 2)
                    bank = R.bank("htok", i)
                    turned("htok", i, [(bank[:, j * P:(j + 1) * P], h[:, 4 * half + j, tok * P:(tok + 1) * P]) for j in range(4)])
                ada(ada_at(R.name, "htok", 0), apart2)
                pe.wait_ge(*slots_ready.take())
                turned("cols", 0, [(R.bank("cols")[0:64, 0:32], seli[0:32, :])])
                pick(nt)
                gather(nt)
                pe.wait_ge(*R.evac("xs", 1))
                flush()

            def gate(b, t, nt):
                c = R.chunk("gate" + b, t // 4)
                if t % 4 == 0:
                    pe.wait_ge(*R.loaded(c))
                from_h("gate" + b, t, c, t % 4, nt)
                if t % 4 == 3:
                    used.append(c)

            def branch(b, nt):
                w = R.chunk("w" + b)
                for t in range(KT):
                    if b == "c" or t >= 2:
                        gate(b, t, nt)
                    if t == 0:
                        pe.wait_ge(*R.loaded(w))
                        pe.wait_ge(*(R.evac("cb", 3) if b == "c" else R.evac("val" + b, len(units(1 if nt == T else 0)) // 2 - 1)))
                    product("br" + b, t, [(R.bank("br" + b, t)[:, 0:nt], [(tile_of(w, k, t, 1024), y2[:, k, 0:nt])
                                                                          for k in range(4)])])
                    if t == KT - 1:
                        used.append(w)
                    ada(ada_at(R.name, b, t), apart2)

            def gqa(layer, n, b):
                us = units(layer)
                for job, i in gqa_heads(layer, b):
                    if job == "gate" + b:
                        gate(b, i, 2 * T if layer == 0 else T)
                    elif job == "s" + b:
                        (s, hd), qt = us[i // 2], i % 2
                        half, kv = hd % 2, hd // 4
                        k = (kf2 if half == kv else kg2)[64 * half:64 * half + 64, n, s * T:2 * T]
                        product(job, i, [(R.bank(job, i)[:, 0:2 * T - s * T], [
                            (qf2[64 * half:64 * half + 64, hd // 2, s * T + qt * P:s * T + (qt + 1) * P], k)])])
                    elif job == "turn" + b:
                        s = us[i // 2][0]
                        pe.wait_ge(*probs_normed.take())
                        turned(job, i, [(R.bank(job, i)[:, k * P:(k + 1) * P], pr2[:, i % 4, k * P:(k + 1) * P])
                                        for k in range(4 - 2 * s)])
                    else:
                        s, hd = us[2 * i]
                        pe.wait_ge(*R.evac("turn" + b, 4 * i + 3))
                        pe.wait_ge(*R.free(job, i))
                        kv, kts = hd // 4, 4 - 2 * s
                        for k in range(kts):
                            for j in range(2):
                                v = vt2[:, k + 2 * s, n * P + kv * 64:n * P + kv * 64 + 64]
                                mm(R.bank(job, i)[64 * j:64 * j + 64, 0:T], v, pt2[:, j, k * T:(k + 1) * T], k == 0,
                                   k == kts - 1, R.filled(job, i) if j and k == kts - 1 else None)

            def pick(nt):
                pe.wait_ge(*onehot_ready.take())
                turned("pick", 0, [(R.bank("pick")[:, i * P:(i + 1) * P], oh[:, i * P:(i + 1) * P]) for i in range(nt // P)])

            def gather(nt):
                pe.wait_ge(*R.evac("pick"))
                for g in range(2):
                    groups = []
                    for d in range(4):
                        for s in range(nt // T):
                            cols = slots_of(R.bank("xs", g)[:, d * P:(d + 1) * P], s)
                            groups.append((cols, [(htok[:, 2 * s + i, (4 * g + d) * P:(4 * g + d + 1) * P],
                                                   slots_of(pk[:, 2 * s + i], s)) for i in range(2)]))
                    product("xs", g, groups)

            def experts(layer):
                nt = 2 * T if layer == 0 else T
                for e in range(2):
                    pe.wait_ge(*R.free("eg", e))
                    pe.wait_ge(*R.free("eu", e))
                    for i in range(4):
                        c = R.chunk("gu", 4 * e + i)
                        pe.wait_ge(*R.loaded(c))
                        for kk in range(2):
                            k = 2 * i + kk
                            for w, job in enumerate(("eg", "eu")):
                                for n in range(2):
                                    at = kk * 2048 + w * 1024 + n * 512
                                    mm(R.bank(job, e)[64 * n:64 * n + 64, :], xs[:, k, 64 * e:64 * e + 64],
                                       ring[:, c % SLOTS, at:at + 512], k == 0, k == 7,
                                       R.filled(job, e) if n and k == 7 else None)
                        used.append(c)
                for e in range(2):
                    pe.wait_ge(*R.evac("eu", e))
                    turned("eh", e, [(R.bank("eh", e)[:, j * P:(j + 1) * P], ae[:, e, j * P:(j + 1) * P]) for j in range(4)])
                    pe.wait_ge(*R.evac("eh", e))
                    pe.wait_ge(*R.free("ey", e))
                    for kh in range(2):
                        c = R.chunk("dn", 2 * e + kh)
                        pe.wait_ge(*R.loaded(c))
                        for j in range(4):
                            for n in range(2):
                                at = j * 1024 + n * 512
                                mm(R.bank("ey", e)[64 * n:64 * n + 64, :], hte[:, e, j * P + kh * 64:j * P + kh * 64 + 64],
                                   ring[:, c % SLOTS, at:at + 512], kh == j == 0, kh == 1 and j == 3,
                                   R.filled("ey", e) if n and kh and j == 3 else None)
                        used.append(c)
                pick(nt)
                pe.wait_ge(*R.evac("ey", 1))
                pe.wait_ge(*picked_ready.take())
                for t in range(KT):
                    product("scat", t, [(R.bank("scat", t)[:, 0:nt], [(ye[:, t * P:(t + 1) * P], og[:, 0:nt])])])
                gather(nt)
                pe.wait_ge(*R.evac("xs", 1))
                flush()

            for b in range(8):
                pe.sem_inc(R.free_sem[b], 1)
            pe.wait_ge(const_in, 16)
            pe.wait_ge(*c_done.take())
            R.phase("a0")
            ada(plan_ada(), apart)
            with pe.Fori(0, 2) as L:
                book.enter("b1", L)
                R.phase("b1", L)
                first_stack(L)
                book.leave("b1", 2)
            for layer in range(2):
                R.phase(f"d{layer}")
                dense(layer)
                with pe.Fori(0, PAIRS) as p:
                    book.enter(f"e{layer}", p)
                    R.phase(f"e{layer}", p)
                    experts(layer)
                    book.leave(f"e{layer}", PAIRS)

        @block.scalar
        def _(act):
            book.start("ACT")
            A = nc.scalar.activation

            def settle(ins):
                ins.then_inc(*act_step.inc())
                act.wait_ge(*act_step.take())

            def parts(jobs, part):
                for job, i in jobs:
                    if job == "ada_part":
                        act.wait_ge(*R.full(job, i))
                        A(part[:, i % 2], R.bank(job, i)[:, :], ACT.Copy).then_inc(*R.freed(job, i))

            def squares(nt):
                for half in range(2):
                    A(h[:, 4 * half:4 * half + 4, 0:nt], X[:, 4 * half:4 * half + 4, 0:nt], ACT.Square)\
                        .then_inc(*sq_ready.inc())

            def root(m, r, t):
                settle(A(r, m, ACT.Ln))
                settle(A(r, r, ACT.Exp, scale=-0.5))
                A(t, r, ACT.Square).then_inc(*root_ready.inc())

            def shifts(tile0, nt):
                for k in range(KT):
                    for s in range(nt // T):
                        act.wait_ge(*h_scaled.take())
                        A(h[:, k, s * T:(s + 1) * T], h[:, k, s * T:(s + 1) * T], ACT.Identity,
                          bias=mod[:, tile0 + k, s:s + 1]).then_inc(*h_ready.inc())

            def first_stack():
                squares(T)
                act.wait_ge(*R.evac("ss1"))
                root(ms[:, 0], rs[:, 0], sq[:, 0])
                shifts(0, T)
                for j in range(4):
                    act.wait_ge(*R.full("lat", j))
                    bank = R.bank("lat", j)[:, 0:T]
                    A(lat[:, j] if j < 3 else krw, bank, ACT.Identity, bias=q1("b_lat", j))
                    A(latsq[:, j] if j < 3 else sq[:, 10], bank, ACT.Square, bias=q1("b_lat", j)).then_inc(*R.freed("lat", j))
                for job, to in (("qsb", qsb), ("ksb", ksb)):
                    for j in range(4):
                        act.wait_ge(*R.full(job, j))
                        A(to[:, j], R.bank(job, j)[:, 0:T], ACT.Identity, bias=q1("b_" + job, j)).then_inc(*R.freed(job, j))
                    if job == "qsb":
                        act.wait_ge(*R.evac("sslat"))
                        root(ms[:, 0:2], rs[:, 0:2], sq[:, 0:2])
                act.wait_ge(*R.evac("z", H1 - 1))
                settle(A(sp[:, :, :], zm[:, :, :], ACT.Abs))
                settle(A(sp[:, :, :], sp[:, :, :], ACT.Exp, scale=-1.0))
                A(sp[:, :, :], sp[:, :, :], ACT.Ln, bias=1.0).then_inc(*log_ready.inc())
                for j in range(10):
                    job, i, to, s = ("q", j, qf, j) if j < 6 else ("k", j - 6, kf, j)
                    act.wait_ge(*R.full(job, i))
                    bank = R.bank(job, i)[:, 0:T]
                    A(to[:, i], bank, ACT.Copy)
                    A(sq[:, s], bank, ACT.Square).then_inc(*R.freed(job, i))
                for job in ("ssq", "ssk"):
                    act.wait_ge(*R.evac(job, 2))
                    root(ms[:, :, :], rs[:, :, :], sq[:, 0:6])
                for i in range(H1):
                    act.wait_ge(*R.evac("cum", i))
                    A(sp[:, i], zm[:, i], ACT.Exp).then_inc(*sb_ready.inc())
                for i in range(H1):
                    act.wait_ge(*R.full("sb_v", i))
                    A(ysb[:, i], R.bank("sb_v", i)[:, 0:T], ACT.Copy).then_inc(*R.freed("sb_v", i))
                def both_gates(t):
                    act.wait_ge(*R.full("gates", t))
                    if t >= 2:
                        act.wait_ge(*R.evac("br", t - 2))
                    bank = R.bank("gates", t)
                    A(sig1[:, t % 2, 0:T], bank[:, 0:T], ACT.Sigmoid, bias=q1("b_gm", t))
                    A(sig1[:, t % 2, T:512], bank[:, T:512], ACT.Sigmoid, bias=q1("b_gs", t)).then_inc(*R.freed("gates", t))

                for job, i in mla_heads():
                    if job == "gates":
                        both_gates(i)
                    elif job == "s":
                        n, u = (i % 2 + 1) * P, i % 4
                        act.wait_ge(*top_ready.take())
                        A(sc1[:, u, 0:n], sc1[:, u, 0:n], ACT.Exp, bias=small[:, 4 + u:5 + u],
                          accum_out=small[:, 8 + u:9 + u]).then_inc(*probs_ready.inc())
                    elif job == "turn":
                        act.wait_ge(*R.full("turn", i))
                        A(pt1[:, i % 2], R.bank("turn", i)[:, 0:384], ACT.Copy).then_inc(*R.freed("turn", i))
                    else:
                        act.wait_ge(*R.full("mla_v", i))
                        A(ymla[:, i], R.bank("mla_v", i)[:, 0:T], ACT.Copy).then_inc(*R.freed("mla_v", i))
                for t in range(2, KT):
                    both_gates(t)
                act.wait_ge(*R.evac("out", KT - 1))
                squares(T)
                act.wait_ge(*R.evac("ss2"))
                root(ms[:, 0], rs[:, 0], ms[:, 2])
                shifts(24, T)
                for p in range(FT + 1):
                    if p < FT:
                        if p % 2 == 0:
                            parts([("ada_part", p // 2)], apart)
                        act.wait_ge(*R.full("up", p))
                        if p >= 3:
                            act.wait_ge(*hid_ready.take())
                        bank, cv = R.bank("up", p), conv1[:, p % 3]
                        for half in range(2):
                            i = half * FT + p
                            ins = A(cv[:, half * T:(half + 1) * T], bank[:, half * T:(half + 1) * T], ACT.Identity,
                                    scale=q1("cw", 2 * 2 * FT + i), bias=q1("cb", i))
                        ins.then_inc(*conv_ready.inc())
                    if p:
                        act.wait_ge(*R.evac("up", p - 1))
                        A(sg1[:, (p - 1) % 2], conv1[:, (p - 1) % 3, 0:T], ACT.Sigmoid).then_inc(*gate_ready.inc())
                parts([("ada_part", 11)], apart)
                act.wait_ge(*hid_ready.take(3))
                act.wait_ge(*R.evac("down", KT - 1))

            def dense(layer):
                nt = 2 * T if layer == 0 else T
                squares(2 * T)
                act.wait_ge(*R.evac("ss1"))
                root(ms2[:, 0], rs2[:, 0], sq2[:, 1])
                shifts(0, 2 * T)
                for job, i in norm_jobs():
                    if (job, i) in NORMED:
                        n = NORMED.index((job, i))
                        w = 2 * T if n < 2 else nt
                        act.wait_ge(*R.full(job, i))
                        A(raw2[n][:, 0:w], R.bank(job, i)[:, 0:w], ACT.Copy)
                        A(sq2[:, n % 4, 0:w], R.bank(job, i)[:, 0:w], ACT.Square).then_inc(*R.freed(job, i))
                    elif job == "vv":
                        act.wait_ge(*R.full("vv", i))
                        A(vt2[:, 2 * i:2 * i + 2], R.bank("vv", i)[:, :].rearrange("p (a n) -> p a n", a=2), ACT.Copy)\
                            .then_inc(*R.freed("vv", i))
                    elif job == "ss":
                        w = 2 * T if i < 2 else nt
                        act.wait_ge(*R.evac("ss", i))
                        if i >= 2:
                            act.wait_ge(*(k_scaled if i < 4 else q_scaled).take())
                        root(ms2[:, i % 2, 0:w], rs2[:, i % 2, 0:w], sq2[:, i % 4, 0:w])
                    elif job == "khalf":
                        act.wait_ge(*R.full("khalf", i))
                        A(kg2[:, i], R.bank("khalf", i)[:, :], ACT.Copy).then_inc(*R.freed("khalf", i))
                q_scaled.skip(2)
                for n, b in enumerate("ab"):
                    us = units(layer)
                    for job, i in gqa_heads(layer, b):
                        if job == "gate" + b:
                            gate(b, i, nt)
                        elif job == "s" + b:
                            s, hd = us[i // 2]
                            w, u = 2 * T - s * T, i % 4
                            act.wait_ge(*top_ready.take())
                            if b == "b":
                                A(small[:, 16 + u:17 + u], q2(layer, "sink", hd), ACT.Exp, bias=small[:, 4 + u:5 + u])
                            if b == "b" and s == 0:
                                A(pr2[:, u, 0:w], pr2[:, u, 0:w], ACT.Exp, bias=small[:, 4 + u:5 + u],
                                  accum_out=small[:, 8 + u:9 + u]).then_inc(*probs_ready.inc())
                            else:
                                A(pr2[:, u, 0:w], R.bank(job, i)[:, 0:w], ACT.Exp, bias=small[:, 4 + u:5 + u], scale=SC_B,
                                  accum_out=small[:, 8 + u:9 + u]).then_inc(*R.freed(job, i))
                        elif job == "turn" + b:
                            s, kts = us[i // 2][0], 4 - 2 * us[i // 2][0]
                            act.wait_ge(*R.full(job, i))
                            to = pt2[:, (i // 2) % 2, 0:kts * T].rearrange("p (k q) -> p k q", k=kts)
                            A(to[:, :, (i % 2) * P:(i % 2 + 1) * P],
                              R.bank(job, i)[:, 0:kts * P].rearrange("p (k q) -> p k q", k=kts), ACT.Copy)\
                                .then_inc(*R.freed(job, i))
                        else:
                            s, hd = us[2 * i]
                            act.wait_ge(*R.full(job, i))
                            A(y2[:, hd // 2, s * T:(s + 1) * T], R.bank(job, i)[:, 0:T], ACT.Copy).then_inc(*R.freed(job, i))
                    gates(b, nt)
                for t in range(4):
                    act.wait_ge(*R.full("cx", t))
                    if t >= 2:
                        act.wait_ge(*R.evac("cb", t - 2))
                    A(xs2c[:, t % 2, 0:nt], R.bank("cx", t)[:, 0:nt], ACT.Copy).then_inc(*R.freed("cx", t))
                    parts(ada_at(R.name, "cx", t), apart2)
                act.wait_ge(*R.evac("cb", 3))
                gates("c", nt)
                act.wait_ge(*R.evac("out", KT - 1))
                squares(nt)
                act.wait_ge(*R.evac("ss2"))
                root(ms2[:, 0, 0:nt], rs2[:, 0, 0:nt], sq2[:, 1, 0:nt])
                shifts(24, nt)
                parts(ada_at(R.name, "norm", 0), apart2)
                act.wait_ge(*logits_ready.take())
                A(lg[:, 0:nt // P], lg[:, 0:nt // P], ACT.Exp).then_inc(*probs_ready.inc())
                parts(ada_at(R.name, "logit", 0), apart2)
                for i in range(2 * nt // P):
                    tok, half = divmod(i, 2)
                    act.wait_ge(*R.full("htok", i))
                    A(htok[:, tok, half * 512:(half + 1) * 512], R.bank("htok", i)[:, :], ACT.Copy).then_inc(*R.freed("htok", i))
                picked(nt)

            def gate(b, t, nt):
                act.wait_ge(*R.full("gate" + b, t))
                if t >= 2:
                    act.wait_ge(*R.evac("br" + b, t - 2))
                A(sig2[:, t % 2, 0:nt], R.bank("gate" + b, t)[:, 0:nt], ACT.Sigmoid).then_inc(*R.freed("gate" + b, t))

            def gates(b, nt):
                for t in range(KT):
                    if b == "c" or t >= 2:
                        gate(b, t, nt)
                    parts(ada_at(R.name, b, t), apart2)
                act.wait_ge(*R.evac("br" + b, KT - 1))

            def picked(nt):
                act.wait_ge(*R.full("pick"))
                A(pk[:, 0:nt // P], R.bank("pick")[:, 0:nt].rearrange("p (t s) -> p t s", s=P), ACT.Copy).then_inc(*R.freed("pick"))

            def experts(layer):
                nt = 2 * T if layer == 0 else T
                for e in range(2):
                    act.wait_ge(*R.full("eg", e))
                    A(sge[:, e], R.bank("eg", e)[:, :], ACT.Sigmoid).then_inc(*egate_ready.inc())
                for e in range(2):
                    act.wait_ge(*R.full("eh", e))
                    A(hte[:, e], R.bank("eh", e)[:, :], ACT.Copy).then_inc(*R.freed("eh", e))
                    act.wait_ge(*R.full("ey", e))
                    A(ye[64 * e:64 * e + 64, 0:512], R.bank("ey", e)[0:64, :], ACT.Copy)
                    A(ye[64 * e:64 * e + 64, 512:1024], R.bank("ey", e)[64:128, :], ACT.Copy).then_inc(*R.freed("ey", e))
                picked(nt)

            act.wait_ge(c_in, 16)
            A(csig[:, :], craw[:, :], ACT.Sigmoid).then_inc(*c_ready.inc())
            R.phase("a0")
            parts(plan_ada()[:17], apart)
            for n in range(2):
                act.wait_ge(*angle_ready.take())
                A(trig[:, n], ang[:, 1 + n], ACT.Sin).then_inc(*root_ready.inc())
            parts(plan_ada()[17:], apart)
            act.wait_ge(x_in, 16)
            act.wait_ge(par_in, 32)
            with act.Fori(0, 2) as L:
                book.enter("b1", L)
                R.phase("b1", L)
                first_stack()
                book.leave("b1", 2)
            act.wait_ge(second_in, 48)
            for layer in range(2):
                R.phase(f"d{layer}")
                dense(layer)
                with act.Fori(0, PAIRS) as p:
                    book.enter(f"e{layer}", p)
                    R.phase(f"e{layer}", p)
                    experts(layer)
                    book.leave(f"e{layer}", PAIRS)
                R.phase(f"e{layer}", PAIRS - 1)
                act.wait_ge(*R.evac("scat", KT - 1))

        @block.vector
        def _(dve):
            book.start("DVE")
            TS, TT, STT = nc.vector.tensor_scalar, nc.vector.tensor_tensor, nc.vector.scalar_tensor_tensor

            def settle(ins):
                ins.then_inc(*dve_step.inc())
                dve.wait_ge(*dve_step.take())

            def wide(a, n=2):
                return a.unsqueeze(1).to_broadcast([P, n, a.shape[1]])

            def columns(jobs):
                for job, i in jobs:
                    if job == "ada_col":
                        dve.wait_ge(*R.full(job, i))
                        nc.vector.tensor_copy(mod_next[:, 4 * i:4 * i + 4].rearrange("p a b -> p (a b)"), R.bank(job, i)[:, 0:8])\
                            .then_inc(*R.freed(job, i))

            def modulation(b_ada, g, tile0):
                settle(TT(mod[:, :], mod_next[:, :], b_ada.unsqueeze(2).to_broadcast([P, 48, 2]), ALU.add))
                gain(g, tile0)

            def gain(g, tile0):
                settle(STT(gains[:, :, :], mod[:, tile0:tile0 + 8], 1.0, g.unsqueeze(2).to_broadcast([P, KT, 2]), ALU.add, ALU.mult))

            def mean(m, bank, n, job, i=0):
                return TS(m, bank, 1.0 / n, EPS, ALU.mult, ALU.add)

            def newton(m, r, t):
                dve.wait_ge(*root_ready.take())
                settle(STT(t, t, -0.5, m, ALU.mult, ALU.mult))
                settle(STT(r, t, 1.5, r, ALU.add, ALU.mult))

            def norm(job, m, r, t, nt):
                dve.wait_ge(*R.full(job))
                mean(m, R.bank(job)[:, 0:nt], D, job).then_inc(*R.freed(job))
                dve.wait_ge(*R.evac(job))
                newton(m, r, t)
                for k in range(KT):
                    for s in range(nt // T):
                        STT(h[:, k, s * T:(s + 1) * T], X[:, k, s * T:(s + 1) * T], gains[:, k, s:s + 1],
                            r[:, s * T:(s + 1) * T], ALU.mult, ALU.mult).then_inc(*h_scaled.inc())

            def residual(job, tile0, streams):
                for t in range(KT):
                    if (job, t) == ("down", 4):
                        columns([("ada_col", 11)])
                    dve.wait_ge(*R.full(job, t))
                    for s in range(streams):
                        c = slice(s * T, (s + 1) * T)
                        ins = STT(X[:, t, c], R.bank(job, t)[:, c], mod[:, tile0 + t, s:s + 1], X[:, t, c], ALU.mult, ALU.add)
                    ins.then_inc(*R.freed(job, t))
                dve.wait_ge(*R.evac(job, KT - 1))

            def first_stack(L):
                nc.vector.tensor_copy(cact[:, :, 0:2], silc[:, bass.ds(L, 1)].rearrange("p a k s -> p (a k) s"))
                settle(nc.vector.tensor_copy(p1[:, :], pars1[:, bass.ds(L, 1), :].rearrange("p a n -> p (a n)")))
                modulation(q1("b_ada", 0, 48), q1("g1", 0, 8), 8)
                norm("ss1", ms[:, 0], rs[:, 0], sq[:, 0], T)
                dve.wait_ge(*R.full("sslat"))
                mean(ms[:, 0], R.bank("sslat")[:, 0:T], 256, "sslat")
                mean(ms[:, 1], R.bank("sslat")[:, T:512], 128, "sslat").then_inc(*R.freed("sslat"))
                dve.wait_ge(*R.evac("sslat"))
                newton(ms[:, 0:2], rs[:, 0:2], sq[:, 0:2])
                for j in range(3):
                    ins = STT(lat[:, j], lat[:, j], q1("g_qlat", j) if j < 2 else q1("g_kvlat"), rs[:, j // 2], ALU.mult, ALU.mult)
                ins.then_inc(*lat_ready.inc())
                for i in range(H1):
                    dve.wait_ge(*R.full("z", i))
                    STT(zm[:, i], R.bank("z", i)[:, 0:384], SC_SB, const_of("past"), ALU.mult, ALU.add).then_inc(*R.freed("z", i))
                dve.wait_ge(*R.evac("z", H1 - 1))
                dve.wait_ge(*log_ready.take())
                STT(sp[:, :, :], zm[:, :, :], 0.0, sp[:, :, :], ALU.max, ALU.add).then_inc(*softplus_ready.inc())
                for i in range(2):
                    dve.wait_ge(*R.full("vmla", i))
                    nc.vector.tensor_copy(vmla[:, i], R.bank("vmla", i)[:, :]).then_inc(*R.freed("vmla", i))
                for job, f, g, ready in (("ssq", qf, "gq", q_scaled), ("ssk", kf, "gk", k_scaled)):
                    for m in range(3):
                        dve.wait_ge(*R.full(job, m))
                        mean(ms[:, 2 * m:2 * m + 2], R.bank(job, m)[:, :].rearrange("p (a b) -> p a b", a=2), 192, job)\
                            .then_inc(*R.freed(job, m))
                    dve.wait_ge(*R.evac(job, 2))
                    newton(ms[:, :, :], rs[:, :, :], sq[:, 0:6])
                    for j in range(6):
                        src = krw if job == "ssk" and j >= 4 else f[:, j]
                        ins = STT(f[:, j], src, q1(g, j // 4), rs[:, j], ALU.mult, ALU.mult)
                    ins.then_inc(*ready.inc())
                for i in range(2):
                    dve.wait_ge(*R.full("vsb", i))
                    nc.vector.tensor_copy(X[:, 2 * i:2 * i + 2, T:2 * T], R.bank("vsb", i)[:, :].rearrange("p (a b) -> p a b", a=2))\
                        .then_inc(*R.freed("vsb", i))
                for i in range(H1):
                    dve.wait_ge(*R.full("cum", i))
                    TT(zm[:, i], zm[:, i], R.bank("cum", i)[:, 0:384], ALU.subtract).then_inc(*R.freed("cum", i))
                for n, (f, scaled, ready) in enumerate(((qf, q_scaled, q_ready), (kf, k_scaled, k_ready))):
                    dve.wait_ge(*scaled.take())
                    dve.wait_ge(*R.full("swap", n))
                    if n:
                        dve.wait_ge(*q_ready.take())
                    TT(ms[:, 0:2], R.bank("swap", n)[:, :].rearrange("p (a b) -> p a b", a=2), wide(trig[:, 1]), ALU.mult)\
                        .then_inc(*R.freed("swap", n))
                    settle(TT(f[:, 4:6], f[:, 4:6], wide(trig[:, 0]), ALU.mult))
                    dve.wait_ge(*R.evac("swap", n))
                    TT(f[:, 4:6], f[:, 4:6], ms[:, 0:2], ALU.add).then_inc(*ready.inc())

                def scores(i):
                    n, u = (i % 2 + 1) * P, i % 4
                    mask = const_of("causal")[:, T - n:T]
                    dve.wait_ge(*R.full("s", i))
                    STT(sc1[:, u, 0:n], R.bank("s", i)[:, 0:n], SC_MLA, mask, ALU.mult, ALU.add).then_inc(*R.freed("s", i))
                    dve.wait_ge(*R.evac("s", i))
                    settle(nc.vector.tensor_reduce(small[:, u:u + 1], sc1[:, u, 0:n], AX, ALU.max))
                    TS(small[:, 4 + u:5 + u], small[:, u:u + 1], -1.0, None, ALU.mult).then_inc(*top_ready.inc())

                def normed(i):
                    n, u = (i % 2 + 1) * P, i % 4
                    dve.wait_ge(*probs_ready.take())
                    settle(nc.vector.reciprocal(small[:, 12 + u:13 + u], small[:, 8 + u:9 + u]))
                    TS(sc1[:, u, 0:n], sc1[:, u, 0:n], small[:, 12 + u:13 + u], None, ALU.mult).then_inc(*probs_normed.inc())

                for i in range(2 * H1):
                    scores(i)
                    if i:
                        normed(i - 1)
                normed(2 * H1 - 1)
                for t in range(KT):
                    dve.wait_ge(*R.full("br", t))
                    dve.wait_ge(*R.evac("gates", t))
                    TT(tmp1[:, t % 2], R.bank("br", t)[:, :], sig1[:, t % 2], ALU.mult).then_inc(*R.freed("br", t))
                    dve.wait_ge(*R.evac("br", t))
                    TT(merged1[:, t], tmp1[:, t % 2, 0:T], tmp1[:, t % 2, T:512], ALU.add).then_inc(*merged_ready.inc())
                residual("out", 16, 1)
                gain(q1("g2", 0, 8), 32)
                norm("ss2", ms[:, 0], rs[:, 0], ms[:, 2], T)

                def convolve(p):
                    dve.wait_ge(*R.full("up", p))
                    dve.wait_ge(*conv_ready.take())
                    bank, cv = R.bank("up", p), conv1[:, p % 3]
                    for back in (1, 2):
                        for half in range(2):
                            o = half * T
                            ins = STT(cv[:, o + back:o + T], bank[:, o:o + T - back], q1("cw", (2 - back) * 2 * FT + half * FT + p),
                                      cv[:, o + back:o + T], ALU.mult, ALU.add)
                        if back == 1:
                            settle(ins)
                    ins.then_inc(*R.freed("up", p))

                def gated(p):
                    cv = conv1[:, p % 3]
                    dve.wait_ge(*gate_ready.take())
                    dve.wait_ge(*R.evac("up", p))
                    settle(TT(cv[:, 0:T], cv[:, 0:T], sg1[:, p % 2], ALU.mult))
                    TT(hid[:, p], cv[:, 0:T], cv[:, T:512], ALU.mult).then_inc(*hid_ready.inc())

                for p in range(FT):
                    if p % 2:
                        columns([("ada_col", p // 2)])
                    convolve(p)
                    if p:
                        gated(p - 1)
                gated(FT - 1)
                residual("down", 40, 1)

            def turn_tile(f, job, j):
                dve.wait_ge(*R.full(job, j))
                TT(rtmp[:, :], R.bank(job, j)[:, 0:T], const_of("sin"), ALU.mult).then_inc(*R.freed(job, j))
                settle(TT(f, f, const_of("cos"), ALU.mult))
                dve.wait_ge(*R.evac(job, j))
                return TT(f, f, rtmp[:, :], ALU.add)

            def dense(layer):
                nt = 2 * T if layer == 0 else T
                modulation(q2(layer, "b_ada", 0, 48), q2(layer, "g1", 0, 8), 8)
                norm("ss1", ms2[:, 0], rs2[:, 0], sq2[:, 1], 2 * T)
                for job, i in norm_jobs():
                    if job == "ss":
                        w, m = 2 * T if i < 2 else nt, i % 2
                        dve.wait_ge(*R.full("ss", i))
                        mean(ms2[:, m, 0:w], R.bank("ss", i)[:, 0:w], 64, "ss").then_inc(*R.freed("ss", i))
                        dve.wait_ge(*R.evac("ss", i))
                        newton(ms2[:, m, 0:w], rs2[:, m, 0:w], sq2[:, i % 4, 0:w])
                        g = q2(layer, "gk", i) if i < 2 else q2(layer, "gqa" if i < 6 else "gqb")
                        settle_to(STT(raw2[i][:, 0:w], raw2[i][:, 0:w], g, rs2[:, m, 0:w], ALU.mult, ALU.mult),
                                  k_scaled if i < 2 else q_scaled)
                    elif job == "swap":
                        settle_to(turn_tile(raw2[i][:, 0:T], "swap", i), k_ready if i < 2 else q_ready)
                for n, b in enumerate("ab"):
                    us = units(layer)

                    def scores(i):
                        (s, hd), u, job = us[i // 2], i % 4, "s" + b
                        w = 2 * T - s * T
                        bank = R.bank(job, i)
                        dve.wait_ge(*R.full(job, i))
                        if b == "b" and s == 0:
                            STT(pr2[:, u, 0:T], bank[:, 0:T], SC_B, const_of("window", i % 2, T), ALU.mult, ALU.add)
                            TS(pr2[:, u, T:w], bank[:, T:w], SC_B, None, ALU.mult).then_inc(*R.freed(job, i))
                            dve.wait_ge(*R.evac(job, i))
                            settle(nc.vector.tensor_reduce(small[:, u:u + 1], pr2[:, u, 0:w], AX, ALU.max))
                            scale = 1.0
                        else:
                            settle(nc.vector.tensor_reduce(small[:, u:u + 1], bank[:, 0:w], AX, ALU.max))
                            scale = SC_B
                        if b == "b":
                            settle(TS(small[:, u:u + 1], small[:, u:u + 1], scale, q2(layer, "sink", hd), ALU.mult, ALU.max))
                            scale = 1.0
                        TS(small[:, 4 + u:5 + u], small[:, u:u + 1], -scale, None, ALU.mult).then_inc(*top_ready.inc())

                    def normed(i):
                        (s, hd), u = us[i // 2], i % 4
                        w = 2 * T - s * T
                        if b == "b" and s == 0:
                            dve.wait_ge(*probs_ready.take())
                        else:
                            dve.wait_ge(*R.evac("s" + b, i))
                        if b == "b":
                            settle(TT(small[:, 8 + u:9 + u], small[:, 8 + u:9 + u], small[:, 16 + u:17 + u], ALU.add))
                        settle(nc.vector.reciprocal(small[:, 12 + u:13 + u], small[:, 8 + u:9 + u]))
                        TS(pr2[:, u, 0:w], pr2[:, u, 0:w], small[:, 12 + u:13 + u], None, ALU.mult).then_inc(*probs_normed.inc())

                    for i in range(2 * len(us)):
                        scores(i)
                        if i:
                            normed(i - 1)
                    normed(2 * len(us) - 1)
                    if b == "a":
                        settle_to(nc.vector.tensor_copy(qf2[:, :, 0:nt], qb2[:, :, 0:nt]), qb_moved)
                    merge(b, nt)
                for t in range(4):
                    u, o = uc[:, t % 2, 0:nt], tc[:, t % 2, 0:nt]
                    us_, os_ = (a.rearrange("p (s n) -> p s n", n=T) for a in (u, o))
                    dve.wait_ge(*R.full("cc", t))
                    dve.wait_ge(*R.evac("cx", t))
                    TT(u, R.bank("cc", t)[:, 0:nt], xs2c[:, t % 2, 0:nt], ALU.mult).then_inc(*R.freed("cc", t))
                    dve.wait_ge(*R.evac("cc", t))
                    settle(TS(o, u, q2(layer, "cw", 4 + t), None, ALU.mult))
                    settle(STT(os_[:, :, 1:T], us_[:, :, 0:T - 1], q2(layer, "cw", t), os_[:, :, 1:T], ALU.mult, ALU.add))
                    settle(STT(os_[:, :, 0:T - 1], us_[:, :, 1:T], q2(layer, "cw", 8 + t), os_[:, :, 0:T - 1], ALU.mult, ALU.add))
                    dve.wait_ge(*R.full("cb", t))
                    TT(y2[:, t, 0:nt], R.bank("cb", t)[:, 0:nt], o, ALU.mult).then_inc(*R.freed("cb", t))
                    columns(ada_at(R.name, "cx", t))
                merge("c", nt)
                residual("out", 16, nt // T)
                gain(q2(layer, "g2", 0, 8), 32)
                norm("ss2", ms2[:, 0, 0:nt], rs2[:, 0, 0:nt], sq2[:, 1, 0:nt], nt)
                n = nt // P
                dve.wait_ge(*R.full("logit"))
                flat = lg[:, 0:n].rearrange("p a e -> p (a e)")
                nc.vector.tensor_copy(flat, R.bank("logit")[:, 0:16 * n]).then_inc(*R.freed("logit"))
                dve.wait_ge(*R.evac("logit"))
                settle(nc.vector.tensor_reduce(small[:, 0:n], lg[:, 0:n], AX, ALU.max))
                TT(lg[:, 0:n], lg[:, 0:n], small[:, 0:n].unsqueeze(2).to_broadcast([P, n, 16]), ALU.subtract)\
                    .then_inc(*logits_ready.inc())
                dve.wait_ge(*logits_ready.take())
                dve.wait_ge(*probs_ready.take())
                settle(nc.vector.tensor_reduce(small[:, 4:4 + n], lg[:, 0:n], AX, ALU.add))
                settle(nc.vector.reciprocal(small[:, 8:8 + n], small[:, 4:4 + n]))
                if layer:
                    settle(nc.vector.memset(aff[:, :, :], 0.0))
                for s in range(nt // T):
                    ins = TT(aff[:, :, 16 * s:16 * s + 16], lg[:, 2 * s:2 * s + 2],
                             small[:, 8 + 2 * s:10 + 2 * s].unsqueeze(2).to_broadcast([P, 2, 16]), ALU.mult)
                ins.then_inc(*affinities_ready.inc())
                columns(ada_at(R.name, "logit", 0))
                dve.wait_ge(*R.full("afft"))
                nc.vector.tensor_copy(wk[0:32, :], R.bank("afft")[0:32, 0:T]).then_inc(*R.freed("afft"))
                dve.wait_ge(*R.evac("afft"))
                for r in range(4):
                    best = seli[0:32, 32 + 8 * r:40 + 8 * r]
                    settle(nc.vector.max(best, wk[0:32, :]))
                    nc.vector.max_index(eidx[0:32, 8 * r:8 * r + 8], best, wk[0:32, :])
                    settle(nc.vector.match_replace(wk[0:32, :], best, wk[0:32, :], -1.0))
                (TS(seli[0:32, 0:32], eidx[0:32, :], 1.0, const_of("ctxrow")[0:32], ALU.mult, ALU.add)
                 .then_inc(*slots_ready.inc()))
                columns(ada_at(R.name, "htok", 0))
                settle(nc.vector.memset(idxc[:, :], 0.0))
                dve.wait_ge(*R.full("cols"))
                bank = R.bank("cols")
                for e in range(2):
                    for s in range(2):
                        q = 64 * e + 32 * s
                        for to, r0 in ((idxc, 0), (gatec, 32)):
                            ins = nc.vector.tensor_copy(to[q:q + 32, 0:PAIRS], bank[r0:r0 + 32, 16 * s + e:16 * s + 16:2])
                ins.then_inc(*R.freed("cols"))
                dve.wait_ge(*R.evac("cols"))
                onehot(nt, idxc[:, 0:1])
                gathered(nt, layer)

            def settle_to(ins, signal):
                ins.then_inc(*signal.inc())
                dve.wait_ge(*signal.take())

            def merge(b, nt):
                for t in range(KT):
                    dve.wait_ge(*R.full("br" + b, t))
                    dve.wait_ge(*R.evac("gate" + b, t))
                    to = merged2[:, t, 0:nt] if b == "a" else tmp2[:, t % 2, 0:nt]
                    TT(to, R.bank("br" + b, t)[:, 0:nt], sig2[:, t % 2, 0:nt], ALU.mult).then_inc(*R.freed("br" + b, t))
                    if b != "a":
                        dve.wait_ge(*R.evac("br" + b, t))
                        ins = TT(merged2[:, t, 0:nt], merged2[:, t, 0:nt], tmp2[:, t % 2, 0:nt], ALU.add)
                        if b == "b":
                            settle(ins)
                        else:
                            ins.then_inc(*merged_ready.inc())
                    columns(ada_at(R.name, b, t))
                if b == "a":
                    dve.wait_ge(*R.evac("bra", KT - 1))

            def onehot(nt, idx):
                TS(oh[:, 0:nt], const_of("iota")[:, 0:nt], idx, None, ALU.is_equal).then_inc(*onehot_ready.inc())

            def gathered(nt, clear=False):
                if clear:
                    settle(nc.vector.memset(xs[:, :, :], 0.0))
                for g in range(2):
                    dve.wait_ge(*R.full("xs", g))
                    to, bank = xs[:, 4 * g:4 * g + 4], R.bank("xs", g)
                    if nt == 2 * T:
                        ins = nc.vector.tensor_copy(to, bank[:, :].rearrange("p (k s) -> p k s", k=4))
                    else:
                        ins = nc.vector.tensor_copy(slots_of(to.rearrange("p k s -> p (k s)"), 0), slots_of(bank[:, :], 0))
                    ins.then_inc(*R.freed("xs", g))

            def experts(layer, p):
                nt = 2 * T if layer == 0 else T
                iota = const_of("iota")[:, 0:nt]
                onehot(nt, idxc[:, bass.ds(p + 1, 1)])
                TS(og[:, 0:nt], iota, idxc[:, bass.ds(p, 1)], gatec[:, bass.ds(p, 1)], ALU.is_equal, ALU.mult)\
                    .then_inc(*picked_ready.inc())
                for e in range(2):
                    dve.wait_ge(*egate_ready.take())
                    TT(ae[:, e], R.bank("eg", e)[:, :], sge[:, e], ALU.mult).then_inc(*R.freed("eg", e))
                    dve.wait_ge(*R.evac("eg", e))
                    dve.wait_ge(*R.full("eu", e))
                    TT(ae[:, e], R.bank("eu", e)[:, :], ae[:, e], ALU.mult).then_inc(*R.freed("eu", e))
                residual("scat", 40, nt // T)
                gathered(nt)

            settle(nc.vector.memset(cact[:, :, :], 0.0))
            dve.wait_ge(*c_ready.take())
            settle(TT(silc[:, :, :, :], craw[:, :].rearrange("p (b k s) -> p b k s", b=2, k=KT),
               csig[:, :].rearrange("p (b k s) -> p b k s", b=2, k=KT), ALU.mult))
            nc.vector.tensor_copy(cact[:, :, 0:2], silc[:, 0]).then_inc(*c_done.inc())
            R.phase("a0")
            columns(plan_ada()[:17])
            dve.wait_ge(const_in, 16)
            dve.wait_ge(pos_in, 16)
            settle(nc.vector.tensor_copy(ang[:, 0], posi[:, :]))
            settle(TS(ang[:, 0], ang[:, 0], const_of("freq"), None, ALU.mult))
            for n, (turns, start) in enumerate(((0.25, np.pi / 2), (0.0, 0.0))):
                k, a = ang[:, 3], ang[:, 1 + n]
                settle(TS(k, ang[:, 0], 1 / (2 * np.pi), turns, ALU.mult, ALU.add))
                settle(TS(k, k, ROUND, None, ALU.add))
                settle(TS(k, k, ROUND, None, ALU.subtract))
                settle(STT(a, k, -TWO_PI[0], ang[:, 0], ALU.mult, ALU.add))
                settle(STT(a, k, -TWO_PI[1], a, ALU.mult, ALU.add))
                settle(STT(a, k, -TWO_PI[2], a, ALU.mult, ALU.add))
                settle(TS(a, a, start, None, ALU.add))
                TS(a, a, 3.1415925, -3.1415925, ALU.min, ALU.max).then_inc(*angle_ready.inc())
            dve.wait_ge(*root_ready.take(2))
            settle(TS(trig[:, 1], trig[:, 1], const_of("sign"), None, ALU.mult))
            columns(plan_ada()[17:])
            dve.wait_ge(*R.evac("ada_col", 11))
            dve.wait_ge(par_in, 32)
            dve.wait_ge(x_in, 16)
            with dve.Fori(0, 2) as L:
                book.enter("b1", L)
                R.phase("b1", L)
                first_stack(L)
                book.leave("b1", 2)
            dve.wait_ge(second_in, 48)
            for layer in range(2):
                R.phase(f"d{layer}")
                dense(layer)
                with dve.Fori(0, PAIRS) as p:
                    book.enter(f"e{layer}", p)
                    R.phase(f"e{layer}", p)
                    experts(layer, p)
                    book.leave(f"e{layer}", PAIRS)
        book.start("end")
        return book.seen, book.totals


def feature_cols(v):
    v = np.asarray(v)
    return v.reshape(*v.shape[:-1], -1, P).transpose(v.ndim, *range(v.ndim))


def chunked(w, cols):
    k = w.shape[0] // P
    return w.reshape(k, P, -1, cols).transpose(2, 1, 0, 3).reshape(-1, P, k * cols)


def padded(a):
    out = np.zeros((a.shape[0], P, CH), a.dtype)
    out[:, :, :a.shape[2]] = a
    return out


def chunks_of(i, stack, l):
    out = {}

    def put(name, a):
        out.update({(name, n): c for n, c in enumerate(a)})

    if stack == 1:
        w = i["w_in"][l]
        put("lat", chunked(np.concatenate([w[:, 0:448], w[:, 384:448]], 1), 512))
        for name, a in (("qsb", 448), ("ksb", 960), ("vsb", 1472)):
            put(name, chunked(w[:, a:a + 512], 512))
        uq = i["w_uq"][l].reshape(256, 4, 192)
        uq = np.concatenate([uq[:, :, :128].reshape(256, 512), uq[:, :, 128:].reshape(256, 256)], 1)
        ukv = i["w_ukv"][l].reshape(128, 4, 2, 128).transpose(0, 2, 1, 3).reshape(128, 1024)
        put("low", padded(np.concatenate([chunked(uq, 768), chunked(ukv, 1024)], 2)))
        put("gm", chunked(w[:, 1984:3008], 512))
        put("gs", chunked(w[:, 3008:4032], 512))
        put("wm", chunked(i["w_branch_mla"][l], 1024))
        put("ws", chunked(i["w_branch_sb"][l], 1024))
        put("out", chunked(i["w_out"][l], 512))
        put("up", chunked(i["w_up"][l].reshape(D, 2, 11, 256).transpose(0, 2, 1, 3).reshape(D, 2 * FF), 512))
        put("down", np.concatenate([padded(chunked(i["w_down"][l][a:a + 1024, half:half + 512], 512))
                                    for half in (0, 512) for a in range(0, FF, 1024)]))
        return out
    w, wb = i["w_in_2"][l], i["w_branch_2"][l]
    put("kv", chunked(w[:, 0:512], 512))
    put("qa", chunked(w[:, 512:1024], 512))
    put("qb", chunked(w[:, 1024:1536], 512))
    put("conv", chunked(w[:, 1536:3072].reshape(D, 3, 4, 128)[:, [1, 2, 0]].transpose(0, 2, 1, 3).reshape(D, 1536), 512))
    for n, b in enumerate("abc"):
        put("gate" + b, chunked(w[:, 3072 + n * 1024:3072 + (n + 1) * 1024], 512))
        put("w" + b, chunked(wb[n], 1024))
    put("out", chunked(i["w_out_2"][l], 512))
    put("router", padded(chunked(i["w_router_2"][l], 16)))
    return out


def stream(i):
    ada = [chunked(a, 512) for a in (*i["w_ada"], *i["w_ada_2"])]
    out = [ada[0]]
    for phase, l, stack in (("b1", 0, 1), ("b1", 1, 1), ("d0", 0, 2), ("e0", 0, 0), ("d1", 1, 2), ("e1", 1, 0)):
        if stack:
            named = chunks_of(i, stack, l)
            following = 2 * (stack - 1) + l + 1
            named.update({("ada", n): c for n, c in enumerate(ada[following])} if following < 4 else {})
            out.append(np.stack([named[x] for x in CHUNK_PLANS[phase]]))
            continue
        gu = np.stack([i["w_e_gate_2"][l], i["w_e_up_2"][l]], 2).reshape(E, 4, 2, P, 2 * 1024)
        gu = gu.transpose(0, 1, 3, 2, 4).reshape(PAIRS, 8, P, CH)
        dn = i["w_e_down_2"][l].reshape(E, 2, 4, P, 1024).transpose(0, 1, 3, 2, 4).reshape(PAIRS, 4, P, CH)
        out.append(np.concatenate([gu, dn], 1).reshape(PAIRS * 12, P, CH))
    return np.concatenate(out, 0)


def params(i):
    f = feature_cols
    b = i["b_in"]
    lat = np.concatenate([b[:, 0:448], b[:, 384:448]], 1)
    heads = lambda g: np.concatenate([f(g[:, :128]), f(np.concatenate([g[:, 128:], g[:, 128:]], 1))], -1)
    flat = lambda a: a.reshape(P, 2, -1)
    one = [f(i["b_ada"]), f(i["g_norm1"]), f(lat), f(b[:, 448:960]), f(b[:, 960:1472]), f(b[:, 1984:3008]),
           f(b[:, 3008:4032]), f(i["g_q_lat"]), f(i["g_kv_lat"]), heads(i["g_q_head"]), heads(i["g_k_head"]), f(i["g_norm2"]),
           flat(f(i["w_conv"])), f(i["b_conv"]), np.broadcast_to(b[None, :, 1472:1984], (P, 2, 512))]
    two = lambda g: f(np.concatenate([g, g], 1))
    sink = np.broadcast_to(i["sink_b_2"][None], (P, 2, HB))
    snd = [f(i["b_ada_2"]), f(i["g_mix_2"]), f(i["g_ffn_2"]), two(i["qg_a_2"]), two(i["qg_b_2"]), two(i["kg_a_2"]),
           two(i["kg_b_2"]), sink, flat(f(i["conv_w_2"]))]
    return np.concatenate(one, 2), np.concatenate(snd, 2)


def kernel(**inputs):
    import concourse.bacc as bacc
    from concourse.bass_utils import run_bass_kernel_spmd as run

    i = {k: np.asarray(v) for k, v in inputs.items()}
    cols = lambda v: v.reshape(KT, P).T
    one, two = params(i)
    cs = np.stack([np.stack([cols(i["c"][0]), cols(i["c"][0])], 2), np.stack([cols(i["c_2"][0]), cols(i["c_ctx_2"])], 2)], 1)
    streams = np.stack([i["x"][0], i["ctx_2"][0]])
    arrays = {
        "weights": stream(i), "const": constants(), "par1": one, "par2": two, "c_cols": cs.reshape(P, 32),
        "x_cols": streams.reshape(2, T, KT, P).transpose(3, 0, 2, 1), "positions": i["positions"],
    }
    arrays = {k: np.ascontiguousarray(v) for k, v in arrays.items()}

    def program(per):
        nc = bacc.Bacc("TRN2", target_bir_lowering=False, num_devices=1)
        args = [nc.dram_tensor(k, v.shape, mybir.dt.from_np(v.dtype), kind="ExternalInput").ap() for k, v in arrays.items()]
        out = nc.dram_tensor("out", (P, KT, T), F32, kind="ExternalOutput").ap()
        return nc, two_stacks(nc, *args, out, per)

    nc, _ = program({(loop, name): n for loop, names in PER.items() for name, n in names.items()})
    got = run(nc, [arrays], core_ids=[0]).results[0]["out"]
    return got.transpose(2, 1, 0).reshape(1, T, D)
```
